# Optimizing a Trainium2 kernel written in Bass

```python
import jax, jax.numpy as jnp
from jax import lax
import numpy as np

D_MODEL = 1024
BATCH = 1
SEQ = 256
DEPTH = 2

GRID_W = 64
CTX_LEN = 256

HEAD_DIM = 64
ROPE_BASE = 10000.0
NORM_EPS = 1e-6
GN_EPS = 1e-5
NEG_INF = -1e30

NA_HEADS = D_MODEL // HEAD_DIM // 2
NA_ROWS = 8
NA_COLS = 16
RET_HEADS = D_MODEL // HEAD_DIM // 2
RET_CHUNK = 128
W_A = NA_HEADS * HEAD_DIM
W_B = RET_HEADS * HEAD_DIM
AB_SPLITS = (W_A, 2 * W_A, 3 * W_A, 3 * W_A + W_B, 3 * W_A + 2 * W_B, 3 * W_A + 3 * W_B)
AB_IN = 3 * W_A + 4 * W_B
AB_OUT = W_A + W_B

SWA_Q_HEADS = D_MODEL // HEAD_DIM
SWA_KV_HEADS = 4
SWA_WINDOW = 128
SWA_Q_W = SWA_Q_HEADS * HEAD_DIM
SWA_KV_W = SWA_KV_HEADS * HEAD_DIM
SWA_IN = SWA_Q_W + 2 * SWA_KV_W
SWA_OUT = SWA_Q_W

PEER_HEADS = 8
PEER_KEYS = 128
PEER_EXPERTS = PEER_KEYS * PEER_KEYS
PEER_TOPK = 16
PEER_QDIM = 256
PEER_BLOCK = 128

kernel_name = 'hybrid_na_retention_swa_peer'

def rms_norm(x, g):
    xf = x.astype(jnp.float32)
    y = xf * lax.rsqrt(jnp.mean(xf * xf, axis=-1, keepdims=True) + NORM_EPS)
    return (y * g.astype(jnp.float32)).astype(x.dtype)

def modulate(x, gain, shift, scale):
    return rms_norm(x, gain) * (1.0 + scale) + shift

def adaln(cond, w, b):
    return jnp.split(jax.nn.silu(cond) @ w + b, 6, axis=-1)

def axial_rope(n_tokens, head_dim):
    t = jnp.arange(n_tokens)
    row = (t // GRID_W).astype(jnp.float32)
    col = (t % GRID_W).astype(jnp.float32)
    n_freq = head_dim // 4
    inv_freq = jnp.power(ROPE_BASE, -jnp.arange(n_freq, dtype=jnp.float32) / n_freq)
    ang = jnp.concatenate([row[:, None] * inv_freq, col[:, None] * inv_freq], axis=-1)
    return jnp.cos(ang), jnp.sin(ang)

def apply_rope(x, cos, sin):
    half = x.shape[-1] // 2
    x1, x2 = x[..., :half], x[..., half:]
    c = cos[None, :, None, :].astype(x.dtype)
    s = sin[None, :, None, :].astype(x.dtype)
    return jnp.concatenate([x1 * c - x2 * s, x1 * s + x2 * c], axis=-1)

def context_attention(q, k, v, sink=None):
    B, L, Hq, d = q.shape
    Hkv = k.shape[2]
    G = Hq // Hkv
    s = jnp.einsum('bqkgd,blkd->bkgql', q.reshape(B, L, Hkv, G, d), k).astype(jnp.float32)
    if sink is not None:
        sink_col = jnp.broadcast_to(sink.reshape(Hkv, G, 1, 1).astype(jnp.float32), (B, Hkv, G, L, 1))
        s = jnp.concatenate([s, sink_col], axis=-1)
    p = jax.nn.softmax(s, axis=-1)[..., :L].astype(v.dtype)
    return jnp.einsum('bkgql,blkd->bqkgd', p, v).reshape(B, L, Hq, d)

def neighbourhood_attention(q, k, v, k_ctx, v_ctx, rpb):
    B, S, H, d = q.shape
    rows = S // GRID_W
    kr = min(NA_ROWS, rows)
    n_keys = kr * NA_COLS
    r = jnp.arange(rows)
    col = jnp.arange(GRID_W)
    key_rows = jnp.clip(r - kr // 2, 0, rows - kr)[:, None] + jnp.arange(kr)
    key_cols = jnp.clip(col - NA_COLS // 2, 0, GRID_W - NA_COLS)[:, None] + jnp.arange(NA_COLS)
    key_tok = (key_rows[:, None, :, None] * GRID_W + key_cols[None, :, None, :]).reshape(rows, GRID_W, n_keys)
    dr = key_rows - r[:, None] + (NA_ROWS - 1)
    dc = key_cols - col[:, None] + (NA_COLS - 1)
    bias = rpb[:, dr[:, None, :, None], dc[None, :, None, :]]
    bias = bias.reshape(H, rows, GRID_W, n_keys).transpose(1, 0, 2, 3)
    q_rows = q.reshape(B, rows, GRID_W, H, d).transpose(1, 0, 2, 3, 4)

    def one_row(args):
        q_r, tok_r, bias_r = args
        k_w = k[:, tok_r]
        v_w = v[:, tok_r]
        s_loc = jnp.einsum('bwhd,bwkhd->bhwk', q_r, k_w).astype(jnp.float32) + bias_r.astype(jnp.float32)
        s_ctx = jnp.einsum('bwhd,blhd->bhwl', q_r, k_ctx).astype(jnp.float32)
        p = jax.nn.softmax(jnp.concatenate([s_loc, s_ctx], axis=-1), axis=-1).astype(v.dtype)
        return (jnp.einsum('bhwk,bwkhd->bwhd', p[..., :n_keys], v_w)
                + jnp.einsum('bhwl,blhd->bwhd', p[..., n_keys:], v_ctx))

    out = lax.map(one_row, (q_rows, key_tok, bias))
    return out.transpose(1, 0, 2, 3, 4).reshape(B, S, H, d)

def retention_scan(q, k, v, log_gamma, state0):
    B, T, H, dk = q.shape
    dv = v.shape[-1]
    C = RET_CHUNK
    n = T // C
    to_chunks = lambda t: t.reshape(B, n, C, H, t.shape[-1]).transpose(1, 0, 3, 2, 4)
    i = jnp.arange(C, dtype=jnp.float32)
    diff = i[:, None] - i[None, :]
    lg = log_gamma[:, None, None]
    decay_intra = jnp.where(diff >= 0, jnp.exp(lg * jnp.maximum(diff, 0.0)), 0.0)
    decay_q = jnp.exp(log_gamma[:, None] * (i + 1.0))[None, :, :, None]
    decay_k = jnp.exp(log_gamma[:, None] * (C - 1.0 - i))[None, :, :, None]
    decay_chunk = jnp.exp(log_gamma * C)[None, :, None, None]

    def step(S, xs):
        qb, kb, vb = xs
        intra = jnp.einsum('bhid,bhjd->bhij', qb, kb) * decay_intra
        o = jnp.einsum('bhij,bhjv->bhiv', intra, vb) + jnp.einsum('bhid,bhdv->bhiv', qb * decay_q, S)
        S = S * decay_chunk + jnp.einsum('bhjd,bhjv->bhdv', kb * decay_k, vb)
        return S, o

    S_T, o = lax.scan(step, state0, (to_chunks(q), to_chunks(k), to_chunks(v)))
    return o.transpose(1, 0, 3, 2, 4).reshape(B, T, H, dv), S_T

def bidirectional_retention(q, k, v, log_gamma, state_fwd0, state_bwd0):
    o_f, s_f = retention_scan(q, k, v, log_gamma[0], state_fwd0)
    o_b, s_b = retention_scan(q[:, ::-1], k[:, ::-1], v[:, ::-1], log_gamma[1], state_bwd0)
    diag = jnp.einsum('bthd,bthd->bth', q, k).astype(jnp.float32)[..., None] * v.astype(jnp.float32)
    return o_f + o_b[:, ::-1] - diag, s_f, s_b

def retention_output(o, g):
    mu = jnp.mean(o, axis=-1, keepdims=True)
    oc = o - mu
    on = oc * lax.rsqrt(jnp.mean(oc * oc, axis=-1, keepdims=True) + GN_EPS)
    B, T = o.shape[0], o.shape[1]
    return (on.reshape(B, T, -1) * jax.nn.silu(g.astype(jnp.float32))).astype(g.dtype)

def mixer_na_retention(hx, hc, w_in, w_out, q_norm, k_norm, rpb, ret_log_decay, cos, sin, need_ctx):
    B, S, _ = hx.shape
    L = hc.shape[1]
    scale = HEAD_DIM ** -0.5

    def split(p, T):
        aq, ak, av, bq, bk, bv, bg = jnp.split(p, AB_SPLITS, axis=-1)
        heads = lambda t: t.reshape(B, T, -1, HEAD_DIM)
        return heads(aq), heads(ak), heads(av), heads(bq), heads(bk), heads(bv), bg

    aqx, akx, avx, bqx, bkx, bvx, bgx = split(hx @ w_in, S)
    aqc, akc, avc, bqc, bkc, bvc, bgc = split(hc @ w_in, L)

    aqx = rms_norm(aqx, q_norm) * scale
    akx = rms_norm(akx, k_norm)
    aqc = rms_norm(aqc, q_norm) * scale
    akc = rms_norm(akc, k_norm)
    oa_x = neighbourhood_attention(aqx, akx, avx, akc, avc, rpb)

    log_gamma = -jnp.exp(ret_log_decay.astype(jnp.float32))
    zeros = jnp.zeros((B, RET_HEADS, HEAD_DIM, HEAD_DIM), jnp.float32)
    ob_c, st_f, st_b = bidirectional_retention(bqc * scale, bkc, bvc, log_gamma, zeros, zeros)
    ob_x, _, _ = bidirectional_retention(apply_rope(bqx, cos, sin) * scale, apply_rope(bkx, cos, sin),
                                         bvx, log_gamma, st_f, st_b)

    yx = jnp.concatenate([oa_x.reshape(B, S, -1), retention_output(ob_x, bgx)], axis=-1) @ w_out
    if not need_ctx:
        return yx, None
    oa_c = context_attention(aqc, akc, avc)
    yc = jnp.concatenate([oa_c.reshape(B, L, -1), retention_output(ob_c, bgc)], axis=-1) @ w_out
    return yx, yc

def windowed_gqa(q, k, v, k_ctx, v_ctx, sink):
    B, S, Hq, d = q.shape
    Hkv = k.shape[2]
    G = Hq // Hkv
    L = k_ctx.shape[1]
    blk = SWA_WINDOW
    n = S // blk
    n_loc = 3 * blk

    def key_blocks(t):
        tp = jnp.pad(t, ((0, 0), (blk, blk), (0, 0), (0, 0))).reshape(B, n + 2, blk, Hkv, d)
        tb = jnp.concatenate([tp[:, :-2], tp[:, 1:-1], tp[:, 2:]], axis=2)
        return tb.transpose(1, 0, 2, 3, 4)

    kb, vb = key_blocks(k), key_blocks(v)
    qb = q.reshape(B, n, blk, Hkv, G, d).transpose(1, 0, 2, 3, 4, 5)
    i = jnp.arange(n)
    q_pos = i[:, None] * blk + jnp.arange(blk)[None, :]
    key_pos = i[:, None] * blk - blk + jnp.arange(n_loc)[None, :]
    mask = ((jnp.abs(q_pos[:, :, None] - key_pos[:, None, :]) <= SWA_WINDOW)
            & (key_pos[:, None, :] >= 0) & (key_pos[:, None, :] < S))
    sink_col = jnp.broadcast_to(sink.reshape(Hkv, G, 1, 1).astype(jnp.float32), (B, Hkv, G, blk, 1))

    def one_block(args):
        q_i, k_i, v_i, m_i = args
        s_loc = jnp.where(m_i, jnp.einsum('bqkgd,bskd->bkgqs', q_i, k_i).astype(jnp.float32), NEG_INF)
        s_ctx = jnp.einsum('bqkgd,blkd->bkgql', q_i, k_ctx).astype(jnp.float32)
        p = jax.nn.softmax(jnp.concatenate([s_loc, s_ctx, sink_col], axis=-1), axis=-1).astype(v.dtype)
        return (jnp.einsum('bkgqs,bskd->bqkgd', p[..., :n_loc], v_i)
                + jnp.einsum('bkgql,blkd->bqkgd', p[..., n_loc:n_loc + L], v_ctx))

    out = lax.map(one_block, (qb, kb, vb, mask))
    return out.transpose(1, 0, 2, 3, 4, 5).reshape(B, S, Hq, d)

def mixer_window_gqa(hx, hc, w_in, w_out, q_norm, k_norm, sink, cos, sin, need_ctx):
    B, S, _ = hx.shape
    L = hc.shape[1]
    scale = HEAD_DIM ** -0.5

    def split(p, T):
        q, k, v = jnp.split(p, (SWA_Q_W, SWA_Q_W + SWA_KV_W), axis=-1)
        return (q.reshape(B, T, SWA_Q_HEADS, HEAD_DIM), k.reshape(B, T, SWA_KV_HEADS, HEAD_DIM),
                v.reshape(B, T, SWA_KV_HEADS, HEAD_DIM))

    qx, kx, vx = split(hx @ w_in, S)
    qc, kc, vc = split(hc @ w_in, L)
    qx = apply_rope(rms_norm(qx, q_norm), cos, sin) * scale
    kx = apply_rope(rms_norm(kx, k_norm), cos, sin)
    qc = rms_norm(qc, q_norm) * scale
    kc = rms_norm(kc, k_norm)
    yx = windowed_gqa(qx, kx, vx, kc, vc, sink).reshape(B, S, -1) @ w_out
    if not need_ctx:
        return yx, None
    yc = context_attention(qc, kc, vc, sink).reshape(B, L, -1) @ w_out
    return yx, yc

def peer(h, w_q, sub_keys, u, v):
    B, T, D = h.shape
    q = (h @ w_q).reshape(B, T, PEER_HEADS, 2, PEER_QDIM // 2)
    s = jnp.einsum('bthpd,hpnd->bthpn', q, sub_keys).astype(jnp.float32)
    s1, i1 = lax.top_k(s[..., 0, :], PEER_TOPK)
    s2, i2 = lax.top_k(s[..., 1, :], PEER_TOPK)
    cand_s = (s1[..., :, None] + s2[..., None, :]).reshape(B, T, PEER_HEADS, PEER_TOPK * PEER_TOPK)
    cand_i = (i1[..., :, None] * PEER_KEYS + i2[..., None, :]).reshape(B, T, PEER_HEADS, PEER_TOPK * PEER_TOPK)
    top_s, pos = lax.top_k(cand_s, PEER_TOPK)
    idx = jnp.take_along_axis(cand_i, pos, axis=-1)
    gate = jax.nn.softmax(top_s, axis=-1)
    n_e = PEER_HEADS * PEER_TOPK
    nb = (B * T) // PEER_BLOCK
    hb = h.reshape(nb, PEER_BLOCK, D)
    ib = idx.reshape(nb, PEER_BLOCK, n_e)
    gb = gate.reshape(nb, PEER_BLOCK, n_e)

    def one_block(args):
        h_i, i_i, g_i = args
        act = jax.nn.gelu(jnp.einsum('td,ted->te', h_i, u[i_i]), approximate=False)
        return jnp.einsum('te,ted->td', (g_i * act).astype(h.dtype), v[i_i])

    return lax.map(one_block, (hb, ib, gb)).reshape(B, T, D)

def setup_inputs(seed: int = 0) -> dict:
    key = jax.random.key(seed)
    ks = jax.random.split(key, 24)
    f32 = jnp.float32
    n_even = (DEPTH + 1) // 2
    n_odd = DEPTH // 2
    nrm = lambda k, shape, s: jax.random.normal(k, shape, f32) * s
    base_decay = jnp.log(-jnp.log1p(-jnp.power(2.0, -5.0 - jnp.arange(RET_HEADS, dtype=f32))))
    return {
        'x': nrm(ks[0], (BATCH, SEQ, D_MODEL), 1.0),
        'c': nrm(ks[1], (BATCH, D_MODEL), 1.0),
        'ctx': nrm(ks[2], (BATCH, CTX_LEN, D_MODEL), 1.0),
        'c_ctx': nrm(ks[3], (D_MODEL,), 1.0),
        'mod_w': nrm(ks[4], (DEPTH, D_MODEL, 6 * D_MODEL), D_MODEL ** -0.5),
        'mod_b': nrm(ks[5], (DEPTH, 6 * D_MODEL), 0.02),
        'norm1_g': 1.0 + nrm(ks[6], (DEPTH, D_MODEL), 0.02),
        'norm2_g': 1.0 + nrm(ks[7], (DEPTH, D_MODEL), 0.02),
        'ab_w_in': nrm(ks[8], (n_even, D_MODEL, AB_IN), D_MODEL ** -0.5),
        'ab_w_out': nrm(ks[9], (n_even, AB_OUT, D_MODEL), AB_OUT ** -0.5),
        'na_q_norm': 1.0 + nrm(ks[10], (n_even, HEAD_DIM), 0.02),
        'na_k_norm': 1.0 + nrm(ks[11], (n_even, HEAD_DIM), 0.02),
        'na_rpb': nrm(ks[12], (n_even, NA_HEADS, 2 * NA_ROWS - 1, 2 * NA_COLS - 1), 0.1),
        'ret_log_decay': base_decay[None, None, :] + nrm(ks[13], (n_even, 2, RET_HEADS), 0.05),
        'swa_w_in': nrm(ks[14], (n_odd, D_MODEL, SWA_IN), D_MODEL ** -0.5),
        'swa_w_out': nrm(ks[15], (n_odd, SWA_OUT, D_MODEL), SWA_OUT ** -0.5),
        'swa_q_norm': 1.0 + nrm(ks[16], (n_odd, HEAD_DIM), 0.02),
        'swa_k_norm': 1.0 + nrm(ks[17], (n_odd, HEAD_DIM), 0.02),
        'swa_sink': nrm(ks[18], (n_odd, SWA_Q_HEADS), 0.5),
        'peer_w_q': nrm(ks[19], (DEPTH, D_MODEL, PEER_HEADS * PEER_QDIM), D_MODEL ** -0.5),
        'peer_sub_keys': nrm(ks[20], (DEPTH, PEER_HEADS, 2, PEER_KEYS, PEER_QDIM // 2), (PEER_QDIM // 2) ** -0.5),
        'peer_u': nrm(ks[21], (DEPTH, PEER_EXPERTS, D_MODEL), D_MODEL ** -0.5),
        'peer_v': nrm(ks[22], (DEPTH, PEER_EXPERTS, D_MODEL), 0.5),
    }

def reference(x, c, ctx, c_ctx, mod_w, mod_b, norm1_g, norm2_g, ab_w_in, ab_w_out, na_q_norm, na_k_norm,
              na_rpb, ret_log_decay, swa_w_in, swa_w_out, swa_q_norm, swa_k_norm, swa_sink,
              peer_w_q, peer_sub_keys, peer_u, peer_v):
    S = x.shape[1]
    cos, sin = axial_rope(S, HEAD_DIM)
    x_lat, x_ctx = x, ctx
    for l in range(DEPTH):
        need_ctx = l < DEPTH - 1
        sh1, sc1, g1, sh2, sc2, g2 = [m[:, None, :] for m in adaln(c, mod_w[l], mod_b[l])]
        ch1, cs1, cg1, ch2, cs2, cg2 = adaln(c_ctx, mod_w[l], mod_b[l])
        hx = modulate(x_lat, norm1_g[l], sh1, sc1)
        hc = modulate(x_ctx, norm1_g[l], ch1, cs1)
        j = l // 2
        if l % 2 == 0:
            yx, yc = mixer_na_retention(hx, hc, ab_w_in[j], ab_w_out[j], na_q_norm[j], na_k_norm[j],
                                        na_rpb[j], ret_log_decay[j], cos, sin, need_ctx)
        else:
            yx, yc = mixer_window_gqa(hx, hc, swa_w_in[j], swa_w_out[j], swa_q_norm[j], swa_k_norm[j],
                                      swa_sink[j], cos, sin, need_ctx)
        x_lat = x_lat + g1 * yx
        hx2 = modulate(x_lat, norm2_g[l], sh2, sc2)
        x_lat = x_lat + g2 * peer(hx2, peer_w_q[l], peer_sub_keys[l], peer_u[l], peer_v[l])
        if need_ctx:
            x_ctx = x_ctx + cg1 * yc
            hc2 = modulate(x_ctx, norm2_g[l], ch2, cs2)
            x_ctx = x_ctx + cg2 * peer(hc2, peer_w_q[l], peer_sub_keys[l], peer_u[l], peer_v[l])
    return x_lat


_drawn_inputs = setup_inputs


def setup_inputs(seed=0):
    import zlib

    import numpy as np

    out = dict(_drawn_inputs(seed))
    spreads = {}
    factors = {'na_q_norm': 5.492,
     'na_k_norm': 4.765,
     'na_rpb': 3.386,
     'swa_q_norm': 8.0,
     'swa_k_norm': 8.0,
     'swa_sink': 8.0}
    for name, (base, spread) in spreads.items():
        noise = np.random.default_rng([zlib.crc32(name.encode()), seed]).standard_normal(out[name].shape)
        drawn = base * np.exp(spread * noise) if base else spread * noise
        out[name] = __import__('jax').numpy.asarray(drawn.astype(out[name].dtype))
    for name, factor in factors.items():
        out[name] = (out[name] * factor).astype(out[name].dtype)
    return out
```

```python
from contextlib import ExitStack

import numpy as np

import concourse.bass as bass
from concourse import mybir

ALU = mybir.AluOpType
ACT = mybir.ActivationFunctionType
AX = mybir.AxisListType.X
F32 = mybir.dt.float32
U32 = mybir.dt.uint32

P = 128
D = 1024
KC = D // P
TOK = 256
NT = 2 * TOK // P
HD = 64
GRID_W = 64
NA_ROWS, NA_COLS = 8, 16
WINDOW = 128
NEG = -1e30
LOWEST = -3.4e38
HEADS0 = 8
HEADS1, KV1 = 16, 4
BLK = 512
NW = 2
PH = 8
TOPK = 16
NU = 8
NV = 4

T_ID = 0
T_ROPE = T_ID + P
T_DIST = T_ROPE + 2 * 96
T_MASK = T_DIST + 2 * TOK
T_IOTA = T_MASK + 2 * TOK
T_END = T_IOTA + TOPK


def constant_table():
    t = np.zeros((P, T_END), np.float32)
    t[:, T_ID:T_ID + P] = np.eye(P)
    tok = np.arange(TOK)
    nf = HD // 4
    inv = np.power(10000.0, -np.arange(nf) / nf)
    ang = np.concatenate([(tok // GRID_W)[:, None] * inv, (tok % GRID_W)[:, None] * inv], axis=1)
    rope = np.concatenate([np.cos(ang), -np.sin(ang), np.sin(ang)], axis=1)
    t[:, T_ROPE:T_DIST] = rope.reshape(2, P, 96).transpose(1, 0, 2).reshape(P, 192)
    i, j = np.arange(TOK)[None, :], np.arange(TOK)[:, None]
    t[:, T_DIST:T_MASK] = (i - j).reshape(2, P, TOK).transpose(1, 0, 2).reshape(P, 2 * TOK)
    out = np.abs(i - j) > WINDOW
    t[:, T_MASK:T_IOTA] = np.where(out, NEG, 0.0).reshape(2, P, TOK).transpose(1, 0, 2).reshape(P, 2 * TOK)
    t[:, T_IOTA:] = np.arange(TOPK)
    return t


def bias_places():
    rows = TOK // GRID_W
    kr = min(NA_ROWS, rows)
    t = np.arange(TOK)
    r, c = t // GRID_W, t % GRID_W
    r0 = np.clip(r - kr // 2, 0, rows - kr)
    c0 = np.clip(c - NA_COLS // 2, 0, GRID_W - NA_COLS)
    dr = r[None, :] - r[:, None] + NA_ROWS - 1
    dc = c[None, :] - c[:, None] + NA_COLS - 1
    inside = ((r[None] >= r0[:, None]) & (r[None] < r0[:, None] + kr)
              & (c[None] >= c0[:, None]) & (c[None] < c0[:, None] + NA_COLS))
    return dr, np.where(inside, dc, 2 * NA_COLS - 1)


def backbone(nc, a, out):
    with ExitStack() as ctx:
        def sb(name, shape, dt=F32):
            return ctx.enter_context(nc.sbuf_tensor(name, shape, dt))

        def sem(name):
            return ctx.enter_context(nc.semaphore(name))

        X = sb("resid", [P, NT, D])
        hT = sb("hT", [P, KC, NT * P])
        W = sb("wring", [P, NW, KC, BLK])
        rows = sb("gate_rows", [P, 2, 2, D])
        TB = sb("table", [P, T_END])
        VC = sb("vec_cols", [P, P])
        MC = [sb(f"mod_cols{l}", [P, 48, 2]) for l in range(2)]
        SC = sb("silu_c", [P, 2, KC])
        gains = sb("gains", [P, 4, HD])
        LG = sb("log_gamma", [P, 4, 16])
        sink = sb("sink", [P, 2, HEADS1])
        st = sb("stats", [P, 4, 8])
        sums = sb("sums", [P, 5, 32])
        gst = sb("gn_stats", [P, 4, NT, 8])
        nst = sb("unit_stats", [P, 2, 3, 8])
        IDX = sb("idx", [P, 2, PH * TOPK], U32)
        istage = sb("idx_stage", [P, 2, 2, TOPK], U32)
        GT = sb("gate", [P, 2, PH, TOPK])
        gsm = sb("gate_small", [P, 2, PH])
        rv = sb("route_vals", [P, 3, TOPK])
        ri = sb("route_idx", [P, 5, TOPK], U32)
        rf = sb("route_idx_f", [P, 5, TOPK])
        rs_ = sb("route_s", [P, 4, P])
        rc = sb("route_cand", [P, 2, TOPK * TOPK])
        av_ = sb("act_w", [P, 3, 2, TOPK])
        diag = sb("diag", [P, NV, P])
        ident = TB[:, T_ID:T_ID + P]
        PS = ctx.enter_context(nc.psum_tensor("ps", [P, 8, 512], F32))

        AR = sb("arena", [P, 26112])
        QK0 = AR[:, 0:8192].rearrange("p (w c n) -> p w c n", w=4, c=4)
        V0 = AR[:, 8192:14336].rearrange("p (w t n) -> p w t n", w=3, t=NT)
        O = AR[:, 14336:18432].rearrange("p (t n) -> p t n", t=NT)
        Q1T = AR[:, 0:2048].rearrange("p (c n) -> p c n", c=8)
        K1T = AR[:, 2048:4096].rearrange("p (c n) -> p c n", c=4)
        V1 = AR[:, 8192:9216].rearrange("p (t n) -> p t n", t=NT)
        SQ = AR[:, 18432:19456].rearrange("p (b n) -> p b n", b=2)
        QN = AR[:, 19456:20480].rearrange("p (b n) -> p b n", b=2)
        T1 = AR[:, 20480:20992]
        T2 = AR[:, 20992:21504]
        PB = AR[:, 18432:19456].rearrange("p (b n) -> p b n", b=2)
        PT = AR[:, 19456:20480].rearrange("p (b k n) -> p b k n", b=2, k=4)
        NB = AR[:, 20480:21504].rearrange("p (b t n) -> p b t n", b=2, t=2)
        DC = AR[:, 21504:23552].rearrange("p (b w n) -> p b w n", b=2, w=2)
        ST = AR[:, 18432:21504].rearrange("p (b w n) -> p b w n", b=2, w=3)
        DT = AR[:, 23552:25600].rearrange("p (w n) -> p w n", w=4)
        OC = AR[:, 21504:23552].rearrange("p (t n) -> p t n", t=NT)
        S = AR[:, 0:8192].rearrange("p (t h n) -> p t h n", t=NT, h=16)
        H2 = AR[:, 8192:12288].rearrange("p (t n) -> p t n", t=NT)
        UB = AR[:, 12288:20480].rearrange("p (b n) -> p b n", b=NU)
        VB = AR[:, 20480:24576].rearrange("p (b n) -> p b n", b=NV)
        SK = AR[:, 24064:26112].rearrange("p (h n) -> p h n", h=16)
        rows2 = AR[:, 12288:16384].rearrange("p (c w n) -> p c w n", c=2, w=2)
        QTB = AR[:, 16384:17408].rearrange("p (b n) -> p b n", b=2)
        XN = O
        SK = AR[:, 18432:20480].rearrange("p (h n) -> p h n", h=16)
        TMP = AR[:, 24576:25600]

        ld_tab, ld_x, ld_row, ld_g = sem("ld_tab"), sem("ld_x"), sem("ld_row"), sem("ld_g")
        setup_t, setup_sc, setup_vc = sem("setup_t"), sem("setup_sc"), sem("setup_vc")
        lg_e, lg_done, snk = sem("lg_e"), sem("lg_done"), sem("snk")
        w_in = [sem(f"w_in{i}") for i in range(NW)]
        mod_mm = sem("mod_mm")
        dv = sem("dve_chain")
        L = range(2)
        mc_done = [sem(f"mc_done{l}") for l in L]
        row_mm = sem("row_mm")
        row_ev = sem("row_ev")
        n_ms, n_rt, n_rs = sem("n_ms"), sem("n_rt"), sem("n_rs")
        n1_xn = [sem(f"n1_xn{l}") for l in L]
        n1_tr = [sem(f"n1_tr{l}") for l in L]
        n1_ev = [sem(f"n1_ev{l}") for l in L]
        pr_mm = [sem(f"pr_mm{l}") for l in L]
        pr_free = [sem(f"pr_free{l}") for l in L]
        pr_sq = [sem(f"pr_sq{l}") for l in L]
        pr_ms = [sem(f"pr_ms{l}") for l in L]
        pr_rt = [sem(f"pr_rt{l}") for l in L]
        pr_qn = [sem(f"pr_qn{l}") for l in L]
        pr_tr = [sem(f"pr_tr{l}") for l in L]
        pr_ev = [sem(f"pr_ev{l}") for l in L]
        pr_sg = sem("pr_silu_gate")
        at_s = [sem(f"at_s{l}") for l in L]
        at_max = [sem(f"at_max{l}") for l in L]
        at_exp = [sem(f"at_exp{l}") for l in L]
        at_tr = [sem(f"at_tr{l}") for l in L]
        at_pT = [sem(f"at_pT{l}") for l in L]
        at_pv = [sem(f"at_pv{l}") for l in L]
        at_o = [sem(f"at_o{l}") for l in L]
        nb_in = [sem(f"nb_in{i}") for i in range(2)]
        rt_arg, rt_exp, rt_dc, rt_s = sem("rt_arg"), sem("rt_exp"), sem("rt_dc"), sem("rt_s")
        rt_m, rt_pv, rt_var, rt_sd, rt_o = sem("rt_m"), sem("rt_pv"), sem("rt_var"), sem("rt_sd"), sem("rt_o")
        op_tr = [sem(f"op_tr{l}") for l in L]
        op_ev = [sem(f"op_ev{l}") for l in L]
        op_mm = [sem(f"op_mm{l}") for l in L]
        op_x = [sem(f"op_x{l}") for l in L]
        sk_in = sem("sk_in")
        n2_h = [sem(f"n2_h{l}") for l in L]
        n2_tr = [sem(f"n2_tr{l}") for l in L]
        n2_ev = [sem(f"n2_ev{l}") for l in L]
        pq_mm = [sem(f"pq_mm{l}") for l in L]
        pq_ev = [sem(f"pq_ev{l}") for l in L]
        ps_mm = [sem(f"ps_mm{l}") for l in L]
        ps_ev = [sem(f"ps_ev{l}") for l in L]
        idx_ready, gate_sub, gate_exp = sem("idx_ready"), sem("gate_sub"), sem("gate_exp")
        staged = sem("idx_staged")
        u_in = [sem(f"u_in{i}") for i in range(NU)]
        v_in = [sem(f"v_in{i}") for i in range(NV)]
        u_dot, act_done, w_ready = sem("u_dot"), sem("gelu_done"), sem("w_ready")
        dg_ready, v_used, acc_free = sem("diag_ready"), sem("v_used"), sem("acc_free")
        st_out = sem("st_out")
        apart_pool, apart_dve = sem("apart_pool"), sem("apart_dve")

        tiles = [list(range(NT)), [0, 1]]
        UN = [[(g, t, k) for g, k in enumerate(["q", "k", "v", "rq", "rk", "rv", "gate"]) for t in range(NT)],
              [(g, t, "q") for g in range(2) for t in range(2)] + [(2, t, "kv") for t in range(NT)]]
        NORMED, TURNED = ("q", "k", "kv"), ("q", "k", "kv", "rq", "rk")
        AT = [[(h, t) for h in range(HEADS0) for t in range(NT)], [(h, t) for h in range(HEADS1) for t in range(2)]]
        blocks = []
        for l in L:
            blocks += [("mod", l, b, (mod_mm, 12 * l + b + 1)) for b in range(12)] if l == 0 else []
            n_in = UN[l][-1][0] + 1
            blocks += [("in", l, g, (pr_mm[l], max(i for i, u in enumerate(UN[l]) if u[0] == g) + 1))
                       for g in range(n_in)]
            blocks += [("out", l, b, (op_mm[l], len(tiles[l]) * (b + 1))) for b in range(2)]
            blocks += [("wq", l, b, (pq_mm[l], 4 * (b + 1))) for b in range(4)]
            blocks += [("mod", 1, b, (mod_mm, 12 + b + 1)) for b in range(12)] if l == 0 else []
        place = {(k, l, b): n for n, (k, l, b, _) in enumerate(blocks)}

        def w_wait(eng, kind, l, b):
            n = place[kind, l, b]
            eng.wait_ge(w_in[n % NW], 16 * (n // NW + 1))
            return n % NW

        def index_of(l, u, kinds):
            return sum(k in kinds for _, _, k in UN[l][:u])

        def bcast(ap, shape):
            return ap.broadcast_to(shape)

        PT_ = [(l, t) for l in L for t in tiles[l]]

        block = ctx.enter_context(nc.Block())

        @block.sync
        def _(sp):
            sp.dma_start(TB[:, :], a["table"]).then_inc(ld_tab, 16)
            sp.dma_start(W[0:96, 1, 0, 0:P], a["mod_b"].rearrange("l (j p) -> (l j) p", p=P)).then_inc(ld_row, 16)
            sp.dma_start(W[96:112, 1, 0, 0:P], a["norm1_g"].rearrange("l (j p) -> (l j) p", p=P)).then_inc(ld_row, 16)
            sp.dma_start(W[112:128, 1, 0, 0:P], a["norm2_g"].rearrange("l (j p) -> (l j) p", p=P)).then_inc(ld_row, 16)
            sp.dma_start(W[0:8, 1, 1, 0:P], a["c"].rearrange("b (j p) -> (b j) p", p=P)).then_inc(ld_row, 16)
            sp.dma_start(W[8:16, 1, 1, 0:P], a["c_ctx"].rearrange("(j p) -> j p", p=P)).then_inc(ld_row, 16)
            src = {"mod": lambda l, b: a["mod_w"][l], "in": lambda l, b: (a["ab_w_in"], a["swa_w_in"])[l][0],
                   "out": lambda l, b: (a["ab_w_out"], a["swa_w_out"])[l][0], "wq": lambda l, b: a["peer_w_q"][l]}
            for n, (kind, l, b, _) in enumerate(blocks):
                if n == 1:
                    sp.wait_ge(setup_t, 2)
                if n >= NW:
                    sp.wait_ge(*blocks[n - NW][3])
                sp.dma_start(W[:, n % NW, :, :], src[kind](l, b)[:, b * BLK:(b + 1) * BLK]
                             .rearrange("(k p) n -> p k n", p=P)).then_inc(w_in[n % NW], 16)
                if (kind, l, b) == ("out", 0, 1):
                    for h in range(HEADS0):
                        if h < 2:
                            sp.wait_ge(pr_ev[0], 16)
                        if h >= 2:
                            sp.wait_ge(at_s[0], NT * (h - 2) + 2)
                        sp.dma_start(NB[:, h % 2, :, :], a["nab"][h].rearrange("(t p) n -> p t n", p=P))\
                          .then_inc(nb_in[h % 2], 16)
                if (kind, b) == ("out", 1):
                    sp.wait_ge(op_x[l], 2 * len(tiles[l]))
                    sp.dma_start(SK, a["subk"][l]).then_inc(sk_in, 16)
            sp.wait_ge(acc_free, len(PT_))
            sp.dma_start(out.rearrange("b (t p) d -> p (b t) d", p=P), X[:, 0:2, :]).then_inc(st_out, 16)
            sp.wait_ge(st_out, 16)

        @block.gpsimd
        def _(pool):
            def wait_apart(sem_, value):
                pool.wait_ge(sem_, value)
                pool.sem_inc(apart_pool, 1)

            def gather(table, stage, ring, j, nring, landed):
                nc.gpsimd.indirect_dma_start(
                    out=ring[:, j % nring, :], out_offset=None, in_=table,
                    in_offset=bass.IndirectOffsetOnAxis(ap=stage[:, j:j + 1], axis=0)).then_inc(landed[j % nring], 16)

            def pair(l, g, h, par, hv, parv, b, u, v):
                if u:
                    nc.gpsimd.tensor_copy(istage[:, 0, b, :], IDX[:, par, bass.ds(h * TOPK, TOPK)]).then_inc(staged, 1)
                if v:
                    nc.gpsimd.tensor_copy(istage[:, 1, b, :], IDX[:, parv, bass.ds(hv * TOPK, TOPK)]).then_inc(staged, 1)
                wait_apart(staged, 2 * g + 1 if u else 2 * g)
                for j in range(TOPK):
                    if u:
                        if not (isinstance(g, int) and TOPK * g + j < NU):
                            wait_apart(u_dot, g * TOPK + (j - NU + 1))
                        gather(a[f"peer_u{l}"], istage[:, 0, b, :], UB, j, NU, u_in)
                    if v:
                        if not (isinstance(g, int) and TOPK * (g - 1) + j < NV):
                            wait_apart(v_used, g * TOPK + (j - TOPK - NV + 1))
                        gather(a[f"peer_v{l}"], istage[:, 1, b, :], VB, j, NV, v_in)

            for T, (l, t) in enumerate(PT_):
                first = t == tiles[l][0]
                pool.wait_ge(idx_ready, PH * (T + 1))
                pair(l, 8 * T, 0, T % 2, 7, (T - 1) % 2, 0, True, not first)
                pair(l, 8 * T + 1, 1, T % 2, 0, T % 2, 1, True, True)
                with pool.Fori(1, 4) as i:
                    for e in range(2):
                        pair(l, 8 * T + e + 2 * i, 2 * i + e, T % 2, 2 * i + e - 1, T % 2, e, True, True)
                if t == tiles[l][-1]:
                    pair(l, 8 * T + 8, 0, 0, 7, T % 2, 0, False, True)

        @block.tensor
        def _(pe):
            def turn(dst, src, n=P):
                return nc.tensor.transpose(dst, src, ident[0:n, 0:n])

            def ada(l, b):
                r = w_wait(pe, "mod", l, b)
                for jj in range(4):
                    j = 4 * b + jj
                    for k in range(KC):
                        mm = nc.tensor.matmul(PS[:, 5, 2 * j:2 * j + 2], W[:, r, k, jj * P:(jj + 1) * P],
                                              SC[:, :, k], start=k == 0, stop=k == KC - 1)
                mm.then_inc(mod_mm, 1)

            def row(l, v, c, n):
                if n >= 2:
                    pe.wait_ge(row_ev, n - 1)
                for k in range(KC):
                    at = 2 * (n % 2) + k // 4
                    mm = nc.tensor.matmul(PS[:, at, (k % 4) * P:(k % 4 + 1) * P],
                                          MC[l][:, v * KC + k, c:c + 1].broadcast_to([P, P]), ident,
                                          start=True, stop=True)
                mm.then_inc(row_mm, 1)

            pe.wait_ge(ld_tab, 16)
            pe.wait_ge(ld_row, 80)
            turn(PS[:, 6, 0:P], W[:, 1, 0, 0:P]).then_inc(setup_t, 1)
            turn(PS[:, 7, 0:16], W[0:16, 1, 1, 0:P], 16).then_inc(setup_t, 1)
            pe.wait_ge(setup_sc, 1)
            for b in range(12):
                ada(0, b)
            n_row = 0
            for l in L:
                nt = len(tiles[l])
                pe.wait_ge(mc_done[l], 1)
                for c in range(2 - l):
                    for v in (2, 5):
                        row(l, v, c, n_row)
                        n_row += 1
                for u in range(2 * KC):
                    c, k = divmod(u, KC)
                    pe.wait_ge(n1_xn[l], 2 * c + 2)
                    if u >= 4:
                        pe.wait_ge(n1_ev[l], u - 3)
                    else:
                        pe.wait_ge(row_ev, n_row)
                    for e in range(2):
                        mm = turn(PS[:, u % 4, e * P:(e + 1) * P], XN[:, 2 * c + e, k * P:(k + 1) * P])
                    mm.then_inc(n1_tr[l], 1)
                n1 = len(UN[l])
                for u in range(n1 + 2):
                    if u < n1:
                        g, t, kind = UN[l][u]
                        r = w_wait(pe, "in", l, g)
                        pe.wait_ge(n1_ev[l], 16)
                        if u >= 4:
                            pe.wait_ge(pr_free[l], u - 3)
                        for k in range(KC):
                            mm = nc.tensor.matmul(PS[:, u % 4, :], hT[:, k, t * P:(t + 1) * P], W[:, r, k, :],
                                                  start=k == 0, stop=k == KC - 1)
                        mm.then_inc(pr_mm[l], 1)
                    if u >= 2 and UN[l][u - 2][2] in TURNED:
                        n = index_of(l, u - 2, TURNED)
                        pe.wait_ge(pr_qn[l], n + 1)
                        if n >= 2:
                            pe.wait_ge(pr_ev[l], n - 1)
                        for c in range(4):
                            mm = turn(PS[:, 6 + n % 2, c * P:(c + 1) * P], QN[:, n % 2, c * P:(c + 1) * P])
                        mm.then_inc(pr_tr[l], 1)
                items = AT[l]
                n_items = len(items)
                for i in range(n_items + 2):
                    if i < n_items:
                        h, t = items[i]
                        lo = HD * (h % 2)
                        if l == 0:
                            q, k = QK0[lo:lo + HD, 0, h // 2, t * P:(t + 1) * P], QK0[lo:lo + HD, 1, h // 2, :]
                            if t >= 2:
                                k = k[:, TOK:]
                            pe.wait_ge(nb_in[h % 2], 16 * (h // 2 + 1))
                            bias = NB[:, h % 2, t, :] if t < 2 else None
                        else:
                            q, k = Q1T[lo:lo + HD, h // 2, t * P:(t + 1) * P], K1T[lo:lo + HD, h // 4, :]
                            bias = TB[:, T_MASK + t * TOK:T_MASK + (t + 1) * TOK]
                        if i == 0:
                            pe.wait_ge(pr_ev[l], index_of(l, n1, TURNED))
                            pe.wait_ge(pr_free[l], n1)
                        if i >= 2:
                            pe.wait_ge(at_exp[l], i - 1)
                        if bias is not None:
                            nc.tensor.matmul(PS[:, i % 2, 0:TOK], ident, bias, start=True, stop=False)
                            nc.tensor.matmul(PS[:, i % 2, 0:TOK], q, k[:, 0:TOK], start=False, stop=True)
                            mm = nc.tensor.matmul(PS[:, i % 2, TOK:2 * TOK], q, k[:, TOK:2 * TOK], start=True, stop=True)
                        else:
                            mm = nc.tensor.matmul(PS[:, i % 2, 0:TOK], q, k, start=True, stop=True)
                        mm.then_inc(at_s[l], 1)
                    if 1 <= i <= n_items:
                        m = i - 1
                        nkt = 2 if (l == 0 and items[m][1] >= 2) else 4
                        pe.wait_ge(at_exp[l], m + 1)
                        if m >= 2:
                            pe.wait_ge(at_pT[l], m - 1)
                        for c in range(nkt):
                            mm = turn(PS[:, 2 + m % 2, c * P:(c + 1) * P], PB[:, m % 2, c * P:(c + 1) * P])
                        mm.then_inc(at_tr[l], 1)
                    if i >= 2:
                        m = i - 2
                        h, t = items[m]
                        kts = [2, 3] if (l == 0 and t >= 2) else [0, 1, 2, 3]
                        pe.wait_ge(at_pT[l], m + 1)
                        if m >= 2:
                            pe.wait_ge(at_o[l], m - 1)
                        for c, kt in enumerate(kts):
                            val = V0[:, 0, kt, h * HD:(h + 1) * HD] if l == 0 else V1[:, kt, (h // 4) * HD:(h // 4 + 1) * HD]
                            mm = nc.tensor.matmul(PS[:, 6 + m % 2, 0:HD], PT[:, m % 2, c, :], val,
                                                  start=c == 0, stop=c == len(kts) - 1)
                        mm.then_inc(at_pv[l], 1)
                if l == 0:
                    pe.wait_ge(at_o[0], n_items)
                    for h in range(HEADS0 + 1):
                        if h < HEADS0:
                            lo = HD * (h % 2)
                            if h >= 1:
                                pe.wait_ge(rt_m, 3 * h)
                            for bank, (k0, q0) in enumerate([(2, TOK), (0, 0), (2, 0)]):
                                for e in range(2):
                                    mm = nc.tensor.matmul(
                                        PS[:, bank, e * TOK:(e + 1) * TOK],
                                        QK0[lo:lo + HD, 3, h // 2, (k0 + e) * P:(k0 + e + 1) * P],
                                        QK0[lo:lo + HD, 2, h // 2, q0:q0 + TOK], start=True, stop=True)
                                mm.then_inc(rt_s, 1)
                        if h >= 1:
                            m = h - 1
                            pe.wait_ge(rt_m, 3 * m + 3)
                            for t in range(NT):
                                parts = [(0, 2)] if t >= 2 else [(1, 0), (2, 2)]
                                todo = [(w, e, v0 + e) for w, v0 in parts for e in range(2)]
                                for n, (w, e, kt) in enumerate(todo):
                                    mm = nc.tensor.matmul(
                                        PS[:, 4 + t, m * HD:(m + 1) * HD],
                                        ST[:, m % 2, w, e * TOK + (t % 2) * P:e * TOK + (t % 2) * P + P],
                                        V0[:, 1, kt, m * HD:(m + 1) * HD], start=n == 0, stop=n == len(todo) - 1)
                            mm.then_inc(rt_pv, 1)
                for n in range(2 * nt):
                    t, q = divmod(n, 2)
                    if l == 0:
                        pe.wait_ge(rt_o, t + 1)
                    else:
                        pe.wait_ge(at_o[1], n_items)
                    if n >= 2:
                        pe.wait_ge(op_ev[l], n - 1)
                    for c in range(4):
                        mm = turn(PS[:, n % 2, c * P:(c + 1) * P], O[:, t, (4 * q + c) * P:(4 * q + c + 1) * P])
                    mm.then_inc(op_tr[l], 1)
                pe.wait_ge(op_ev[l], 2 * nt)
                for u in range(2 * nt):
                    b, t = divmod(u, nt)
                    r = w_wait(pe, "out", l, b)
                    if u >= 2:
                        pe.wait_ge(op_x[l], u - 1)
                    for k in range(KC):
                        mm = nc.tensor.matmul(PS[:, 2 + u % 2, :], hT[:, k, t * P:(t + 1) * P], W[:, r, k, :],
                                              start=k == 0, stop=k == KC - 1)
                    mm.then_inc(op_mm[l], 1)
                pe.wait_ge(op_x[l], 2 * nt)
                for c in range(2 - l):
                    for v in (4, 3):
                        row(l, v, c, n_row)
                        n_row += 1
                pe.wait_ge(row_ev, n_row)
                for n in range(2 * nt):
                    t, q = divmod(n, 2)
                    pe.wait_ge(n2_h[l], t + 1)
                    if n >= 2:
                        pe.wait_ge(n2_ev[l], n - 1)
                    for c in range(4):
                        mm = turn(PS[:, n % 2, c * P:(c + 1) * P], H2[:, t, (4 * q + c) * P:(4 * q + c + 1) * P])
                    mm.then_inc(n2_tr[l], 1)
                pe.wait_ge(n2_ev[l], 2 * nt)
                pe.wait_ge(sk_in, 16 * (l + 1))
                for hp in range(17):
                    if hp < 16:
                        r = w_wait(pe, "wq", l, hp // 4)
                        if hp >= 2:
                            pe.wait_ge(pq_ev[l], hp - 1)
                        for k in range(KC):
                            mm = nc.tensor.matmul(PS[:, hp % 2, 0:nt * P], W[:, r, k, (hp % 4) * P:(hp % 4 + 1) * P],
                                                  hT[:, k, 0:nt * P], start=k == 0, stop=k == KC - 1)
                        mm.then_inc(pq_mm[l], 1)
                    if hp >= 1:
                        m = hp - 1
                        pe.wait_ge(pq_ev[l], m + 1)
                        if m >= 2:
                            pe.wait_ge(ps_ev[l], m - 1)
                        for t in range(nt):
                            mm = nc.tensor.matmul(PS[:, 2 + m % 2, t * P:(t + 1) * P], QTB[:, m % 2, t * P:(t + 1) * P],
                                                  SK[:, m, :], start=True, stop=True)
                        mm.then_inc(ps_mm[l], 1)

                def v_head(g, opens):
                    for j in range(TOPK):
                        pe.wait_ge(v_in[j % NV], g * (16 * TOPK // NV) + 16 * (j // NV + 1))
                        pe.wait_ge(dg_ready, g * TOPK + (j + 1))
                        for e in range(2):
                            mm = nc.tensor.matmul(PS[:, 6 + e, :], diag[:, j % NV, :], VB[:, j % NV, e * 512:(e + 1) * 512],
                                                  start=opens and j == 0, stop=False, skip_group_check=True)
                        mm.then_inc(v_used, 1)

                for T, (ll, t) in enumerate(PT_):
                    if ll != l:
                        continue
                    if l == 0:
                        for b in range(3):
                            ada(1, 3 * t + b)
                    if T > 0 and t != tiles[l][0]:
                        pe.wait_ge(acc_free, T)
                    v_head(8 * T, True)
                    v_head(8 * T + 1, False)
                    with pe.Fori(1, 4) as i:
                        for e in range(2):
                            v_head(8 * T + e + 2 * i, False)

        @block.scalar
        def _(act):
            act.dma_start(X[:, 0:2, :], a["x"].rearrange("b (t p) d -> p (b t) d", p=P)).then_inc(ld_x, 16)
            act.dma_start(X[:, 2:4, :], a["ctx"].rearrange("b (t p) d -> p (b t) d", p=P)).then_inc(ld_x, 16)
            for n, name in enumerate(["na_q_norm", "na_k_norm", "swa_q_norm", "swa_k_norm"]):
                act.dma_start(gains[:, n, :], a[name].broadcast_to([P, HD])).then_inc(ld_g, 16)
            act.dma_start(LG[:, 3, :], a["ret_log_decay"].rearrange("a b c -> a (b c)").broadcast_to([P, 16])).then_inc(ld_g, 16)
            act.dma_start(sink[:, 0, :], a["swa_sink"].broadcast_to([P, HEADS1])).then_inc(ld_g, 16)
            act.wait_ge(setup_t, 2)
            nc.scalar.activation(SC[:, :, :], PS[:, 7, 0:16].rearrange("p (c k) -> p c k", c=2), ACT.Silu).then_inc(setup_sc, 1)
            act.wait_ge(ld_g, 96)
            nc.scalar.activation(LG[:, 0, :], LG[:, 3, :], ACT.Exp).then_inc(lg_e, 1)
            n_norm = 0
            n_arg = 0
            for l in L:
                nt = len(tiles[l])
                n1 = len(UN[l])
                act.wait_ge(n_ms, 2 * l + 1)
                nc.scalar.activation(st[:, 2, 0:NT], st[:, 1, 0:NT], ACT.Sqrt).then_inc(n_rt, 1)
                act.wait_ge(n_rs, 2 * l + 1)
                if l == 0:
                    act.wait_ge(ld_x, 32)
                for t in range(NT):
                    nc.scalar.activation(XN[:, t, :], X[:, t, :], ACT.Copy, scale=st[:, 3, t:t + 1]).then_inc(n1_xn[l], 1)
                for u in range(n1 + 3):
                    if u < n1 and UN[l][u][2] in NORMED:
                        n = index_of(l, u, NORMED)
                        wd = 256 if UN[l][u][2] == "kv" else 512
                        act.wait_ge(pr_mm[l], u + 1)
                        if n >= 2:
                            act.wait_ge(pr_ms[l], n - 1)
                            if l == 1:
                                act.wait_ge(pr_qn[l], n - 1)
                        nc.scalar.activation(SQ[:, n % 2, 0:wd], PS[:, u % 4, 0:wd], ACT.Square).then_inc(pr_sq[l], 1)
                    if 1 <= u <= n1 and UN[l][u - 1][2] in NORMED:
                        n = index_of(l, u - 1, NORMED)
                        act.wait_ge(pr_ms[l], n + 1)
                        nc.scalar.activation(nst[:, n % 2, 1, :], nst[:, n % 2, 0, :], ACT.Sqrt).then_inc(pr_rt[l], 1)
                    if 2 <= u <= n1 + 1 and UN[l][u - 2][2] in TURNED:
                        g, t, kind = UN[l][u - 2]
                        n = index_of(l, u - 2, TURNED)
                        act.wait_ge(pr_tr[l], n + 1)
                        if l == 0:
                            dst = QK0[:, {"q": 0, "k": 1, "rq": 2, "rk": 3}[kind], :, t * P:(t + 1) * P]
                        else:
                            dst = (Q1T[:, 4 * g:4 * g + 4, t * P:(t + 1) * P] if kind == "q"
                                   else K1T[:, :, t * P:(t + 1) * P])
                        nc.scalar.activation(dst, PS[:, 6 + n % 2, :].rearrange("p (c n) -> p c n", c=4), ACT.Copy,
                                             scale=HD ** -0.5 if kind in ("q", "rq") else 1.0).then_inc(pr_ev[l], 1)
                if l == 0:
                    act.wait_ge(pr_free[0], n1)
                    nc.scalar.activation(V0[:, 2, :, :], V0[:, 2, :, :], ACT.Silu).then_inc(pr_sg, 1)
                for i, (h, t) in enumerate(AT[l]):
                    nk = TOK if (l == 0 and t >= 2) else 2 * TOK
                    act.wait_ge(at_max[l], i + 1)
                    if i >= 2:
                        act.wait_ge(at_tr[l], i - 1)
                    if i == 0:
                        act.wait_ge(pr_ms[l], index_of(l, n1, NORMED))
                    if l == 1:
                        nc.scalar.activation(sums[:, 2, i:i + 1], sink[:, 0, h:h + 1], ACT.Exp, bias=sums[:, 1, i:i + 1])
                    nc.scalar.activation(PB[:, i % 2, 0:nk], PS[:, i % 2, 0:nk], ACT.Exp, bias=sums[:, 1, i:i + 1],
                                         accum_out=sums[:, 0, i:i + 1]).then_inc(at_exp[l], 1)
                if l == 0:
                    act.wait_ge(lg_done, 1)
                    for h in range(HEADS0):
                        dist = TB[:, T_DIST:T_DIST + 2 * TOK]
                        act.wait_ge(rt_arg, h + 1)
                        if h >= 2:
                            act.wait_ge(rt_m, 3 * (h - 1))
                        if h >= 1:
                            act.wait_ge(rt_dc, h)
                        nc.scalar.activation(DC[:, h % 2, 0, :], DT[:, 0, :], ACT.Exp)
                        nc.scalar.activation(DT[:, 2, :], dist, ACT.Exp, scale=LG[:, 0, h:h + 1], bias=LG[:, 2, h:h + 1])
                        nc.scalar.activation(DT[:, 3, :], dist, ACT.Exp, scale=LG[:, 1, 8 + h:9 + h],
                                             bias=LG[:, 2, 8 + h:9 + h]).then_inc(rt_exp, 1)
                    act.wait_ge(rt_var, 1)
                    nc.scalar.activation(gst[:, 2, :, :], gst[:, 1, :, :], ACT.Sqrt).then_inc(rt_sd, 1)
                for n in range(2 * nt):
                    t, q = divmod(n, 2)
                    act.wait_ge(op_tr[l], n + 1)
                    nc.scalar.activation(hT[:, 4 * q:4 * q + 4, t * P:(t + 1) * P],
                                         PS[:, n % 2, :].rearrange("p (c n) -> p c n", c=4), ACT.Copy).then_inc(op_ev[l], 1)
                act.wait_ge(n_ms, 2 * l + 2)
                nc.scalar.activation(st[:, 2, 0:nt], st[:, 1, 0:nt], ACT.Sqrt).then_inc(n_rt, 1)
                for n in range(2 * nt):
                    t, q = divmod(n, 2)
                    act.wait_ge(n2_tr[l], n + 1)
                    nc.scalar.activation(hT[:, 4 * q:4 * q + 4, t * P:(t + 1) * P],
                                         PS[:, n % 2, :].rearrange("p (c n) -> p c n", c=4), ACT.Copy).then_inc(n2_ev[l], 1)
                for hp in range(16):
                    act.wait_ge(pq_mm[l], hp + 1)
                    if hp >= 2:
                        act.wait_ge(ps_mm[l], hp - 1)
                    nc.scalar.activation(QTB[:, hp % 2, 0:nt * P], PS[:, hp % 2, 0:nt * P], ACT.Copy).then_inc(pq_ev[l], 1)

                def gate_exp_(T):
                    act.wait_ge(gate_sub, T + 1)
                    nc.scalar.activation(GT[:, T % 2, :, :], GT[:, T % 2, :, :], ACT.Exp).then_inc(gate_exp, 1)

                def a_head(g, b):
                    act.wait_ge(u_dot, g * TOPK + TOPK)
                    nc.scalar.activation(av_[:, 1, b, :], av_[:, 0, b, :], ACT.Gelu).then_inc(act_done, 1)
                    act.wait_ge(w_ready, g + 1)
                    for j in range(TOPK):
                        if not (isinstance(g, int) and TOPK * g + j < NV):
                            act.wait_ge(v_used, g * TOPK + (j - NV + 1))
                        nc.scalar.activation(diag[:, j % NV, :], ident, ACT.Copy, scale=av_[:, 2, b, j:j + 1])\
                          .then_inc(dg_ready, 1)

                for T, (ll, t) in enumerate(PT_):
                    if ll != l:
                        continue
                    gate_exp_(T)
                    a_head(8 * T, 0)
                    a_head(8 * T + 1, 1)
                    with act.Fori(1, 4) as i:
                        for e in range(2):
                            a_head(8 * T + e + 2 * i, e)

        @block.vector
        def _(v):
            count = [0]

            def link(ins, apart=False):
                count[0] += 1
                ins.then_inc(dv, 1)
                v.wait_ge(dv, count[0])

            def rms(l, n, nt):
                for t in range(nt):
                    ins = nc.vector.tensor_tensor_reduce(TMP, X[:, t, :], X[:, t, :], 1.0, 0.0, ALU.mult, ALU.add,
                                                         st[:, 0, t:t + 1])
                    link(ins)
                nc.vector.tensor_scalar(st[:, 1, 0:nt], st[:, 0, 0:nt], 1.0 / D, 1e-6, ALU.mult, ALU.add).then_inc(n_ms, 1)
                v.wait_ge(n_rt, n)
                nc.vector.reciprocal(st[:, 3, 0:nt], st[:, 2, 0:nt]).then_inc(n_rs, 1)
                v.wait_ge(n_rs, n)

            def row_evac(dst, n):
                v.wait_ge(row_mm, n + 1)
                at = 2 * (n % 2)
                nc.vector.tensor_copy(dst, PS[:, at:at + 2, :].rearrange("p b n -> p (b n)")).then_inc(row_ev, 1)

            v.wait_ge(setup_t, 1)
            link(nc.vector.tensor_copy(VC[:, :], PS[:, 6, 0:P]))
            v.wait_ge(lg_e, 1)
            link(nc.vector.tensor_scalar(LG[:, 1, :], LG[:, 0, :], 1.0, None, ALU.mult))
            link(nc.vector.tensor_scalar(LG[:, 2, :], LG[:, 0, :], -float(TOK), None, ALU.mult))
            link(nc.vector.tensor_scalar(LG[:, 0, :], LG[:, 0, :], -1.0, None, ALU.mult))
            nc.vector.tensor_scalar(sink[:, 1, :], sink[:, 0, :], -1.0, None, ALU.mult).then_inc(lg_done, 1)
            n_row = 0
            for l in L:
                nt = len(tiles[l])
                n1 = len(UN[l])
                if l == 0:
                    v.wait_ge(ld_x, 32)
                    rms(l, 2 * l + 1, NT)
                v.wait_ge(mod_mm, 12 * (l + 1))
                link(nc.vector.tensor_tensor(MC[l][:, :, :], PS[:, 5, 0:96].rearrange("p (j c) -> p j c", c=2),
                                             VC[:, 48 * l:48 * l + 48].unsqueeze(2).broadcast_to([P, 48, 2]), ALU.add))
                for at, gn in ((8, 96 + 8 * l), (32, 112 + 8 * l)):
                    ins = nc.vector.scalar_tensor_tensor(
                        out=MC[l][:, at:at + 8, :], in0=MC[l][:, at:at + 8, :], scalar=1.0,
                        in1=VC[:, gn:gn + 8].unsqueeze(2).broadcast_to([P, 8, 2]), op0=ALU.add, op1=ALU.mult)
                ins.then_inc(mc_done[l], 1)
                v.wait_ge(mc_done[l], 1)
                for c in range(2 - l):
                    for w in range(2):
                        row_evac(rows[:, c, w, :], n_row)
                        n_row += 1
                if l == 1:
                    rms(l, 2 * l + 1, NT)
                for u in range(2 * KC):
                    c, k = divmod(u, KC)
                    v.wait_ge(n1_tr[l], u + 1)
                    nc.vector.tensor_scalar(hT[:, k, c * TOK:(c + 1) * TOK], PS[:, u % 4, 0:TOK],
                                            MC[l][:, 8 + k, c:c + 1], MC[l][:, k, c:c + 1], ALU.mult, ALU.add)\
                      .then_inc(n1_ev[l], 1)

                def part_a(u):
                    g, t, kind = UN[l][u]
                    n = index_of(l, u, NORMED)
                    nh = 4 if kind == "kv" else 8
                    v.wait_ge(pr_sq[l], n + 1)
                    link(nc.vector.tensor_reduce(nst[:, n % 2, 2, 0:nh], SQ[:, n % 2, 0:nh * HD].rearrange("p (h d) -> p h d", d=HD),
                                                 AX, ALU.add))
                    if nh < 8:
                        link(nc.vector.memset(nst[:, n % 2, 2, nh:8], 1.0))
                    nc.vector.tensor_scalar(nst[:, n % 2, 0, :], nst[:, n % 2, 2, :], 1.0 / HD, 1e-6, ALU.mult, ALU.add)\
                      .then_inc(pr_ms[l], 1)

                def free_psum(u, ins):
                    ins.then_inc(pr_free[l], 1)
                    v.wait_ge(pr_free[l], u + 1)

                def rotated(src, dst, nh, u=None, dup=False):
                    t = UN[l][u][1]
                    r0 = T_ROPE + 96 * t
                    cos = TB[:, r0:r0 + 32].unsqueeze(1).unsqueeze(1).broadcast_to([P, nh, 2, 32])
                    nsin = TB[:, r0 + 32:r0 + 64].unsqueeze(1).broadcast_to([P, nh, 32])
                    sin = TB[:, r0 + 64:r0 + 96].unsqueeze(1).broadcast_to([P, nh, 32])
                    s4 = src.rearrange("p (h e d) -> p h e d", e=2, d=32)
                    t1 = T1[:, 0:nh * HD].rearrange("p (h e d) -> p h e d", e=2, d=32)
                    t2 = T2[:, 0:nh * HD].rearrange("p (h e d) -> p h e d", e=2, d=32)
                    nc.vector.tensor_tensor(t1, s4, cos, ALU.mult)
                    nc.vector.tensor_tensor(t2[:, :, 0, :], s4[:, :, 1, :], nsin, ALU.mult)
                    return nc.vector.tensor_tensor(t2[:, :, 1, :], s4[:, :, 0, :], sin, ALU.mult)

                def doubled(flat, nh):
                    return flat.rearrange("p (h d) -> p h d", d=HD).unsqueeze(2).broadcast_to([P, nh, 2, HD])

                def part_b(u):
                    g, t, kind = UN[l][u]
                    ps = PS[:, u % 4, :]
                    nn, nq = index_of(l, u, NORMED), index_of(l, u, TURNED)
                    if kind in ("v", "rv", "gate"):
                        v.wait_ge(pr_mm[l], u + 1)
                        nc.vector.tensor_copy(V0[:, {"v": 0, "rv": 1, "gate": 2}[kind], t, :], ps).then_inc(pr_free[l], 1)
                        return
                    if nq >= 2:
                        v.wait_ge(pr_tr[l], nq - 1)
                    if nq >= 1:
                        v.wait_ge(pr_qn[l], nq)
                    qn = QN[:, nq % 2, :]
                    if kind in ("rq", "rk"):
                        v.wait_ge(pr_mm[l], u + 1)
                        if t < 2:
                            free_psum(u, rotated(ps, None, 8, u))
                            nc.vector.tensor_tensor(qn, T1, T2, ALU.add).then_inc(pr_qn[l], 1)
                        else:
                            free_psum(u, nc.vector.tensor_copy(qn, ps))
                            nc.vector.sem_inc(pr_qn[l], 1) if False else nc.vector.tensor_copy(T1[:, 0:2], qn[:, 0:2]).then_inc(pr_qn[l], 1)
                        return
                    nh = 4 if kind == "kv" else 8
                    gain = gains[:, 2 * l + (0 if kind == "q" else 1), :]
                    v.wait_ge(pr_rt[l], nn + 1)
                    link(nc.vector.reciprocal(nst[:, nn % 2, 1, 0:nh], nst[:, nn % 2, 1, 0:nh]))
                    if kind == "kv":
                        nc.vector.tensor_copy(V1[:, t, :], ps[:, 256:512])
                    heads = lambda x: x.rearrange("p (h d) -> p h d", d=HD)
                    free_psum(u, nc.vector.tensor_tensor(heads(T2[:, 0:nh * HD]), heads(ps[:, 0:nh * HD]),
                                                         nst[:, nn % 2, 1, 0:nh].unsqueeze(2).broadcast_to([P, nh, HD]), ALU.mult))
                    turned = l == 1 and t < 2
                    gb = gain.unsqueeze(1).broadcast_to([P, nh, HD])
                    if not turned and kind != "kv":
                        nc.vector.tensor_tensor(heads(qn), heads(T2), gb, ALU.mult).then_inc(pr_qn[l], 1)
                        return
                    base = SQ[:, nn % 2, 0:nh * HD]
                    link(nc.vector.tensor_tensor(heads(base), heads(T2[:, 0:nh * HD]), gb, ALU.mult))
                    if kind == "kv":
                        q4 = qn.rearrange("p (h e d) -> p h e d", e=2, d=HD)
                        if turned:
                            link(rotated(base, None, nh, u))
                            ins = [nc.vector.tensor_tensor(q4[:, :, e, :], heads(T1[:, 0:nh * HD]), heads(T2[:, 0:nh * HD]), ALU.add)
                                   for e in range(2)][-1]
                        else:
                            ins = nc.vector.tensor_copy(q4, doubled(base, nh))
                        ins.then_inc(pr_qn[l], 1)
                    else:
                        link(rotated(base, None, nh, u))
                        nc.vector.tensor_tensor(qn, T1, T2, ALU.add).then_inc(pr_qn[l], 1)

                v.wait_ge(ld_g, 96)
                for u in range(n1 + 1):
                    if u < n1 and UN[l][u][2] in NORMED:
                        part_a(u)
                    if u >= 1:
                        part_b(u - 1)

                items = AT[l]
                n_items = len(items)
                for i in range(n_items + 2):
                    if i < n_items:
                        h, t = items[i]
                        nk = TOK if (l == 0 and t >= 2) else 2 * TOK
                        v.wait_ge(at_s[l], i + 1)
                        ins = nc.vector.tensor_reduce(sums[:, 1, i:i + 1], PS[:, i % 2, 0:nk], AX, ALU.max, negate=True)
                        if l == 1:
                            link(ins)
                            ins = nc.vector.tensor_tensor(sums[:, 1, i:i + 1], sums[:, 1, i:i + 1], sink[:, 1, h:h + 1], ALU.min)
                        ins.then_inc(at_max[l], 1)
                    if 1 <= i <= n_items:
                        m = i - 1
                        nk = TOK if (l == 0 and items[m][1] >= 2) else 2 * TOK
                        v.wait_ge(at_tr[l], m + 1)
                        if m >= 2:
                            v.wait_ge(at_pv[l], m - 1)
                        nc.vector.tensor_copy(PT[:, m % 2, 0:nk // P, :], PS[:, 2 + m % 2, 0:nk].rearrange("p (k n) -> p k n", n=P))\
                          .then_inc(at_pT[l], 1)
                    if i >= 2:
                        m = i - 2
                        h, t = items[m]
                        v.wait_ge(at_pv[l], m + 1)
                        if l == 1:
                            link(nc.vector.tensor_tensor(sums[:, 3, m:m + 1], sums[:, 0, m:m + 1], sums[:, 2, m:m + 1], ALU.add))
                        link(nc.vector.reciprocal(sums[:, 4, m:m + 1], sums[:, 3 if l else 0, m:m + 1]))
                        nc.vector.tensor_scalar(O[:, t, h * HD:(h + 1) * HD], PS[:, 6 + m % 2, 0:HD], sums[:, 4, m:m + 1],
                                                None, ALU.mult).then_inc(at_o[l], 1)

                if l == 0:
                    def decay_arg(h):
                        dist = TB[:, T_DIST:T_DIST + 2 * TOK]
                        if h >= 1:
                            v.wait_ge(rt_exp, h)
                        nc.vector.tensor_scalar(DT[:, 0, :], dist, 0.0, LG[:, 0, h:h + 1], ALU.max, ALU.mult)
                        link(nc.vector.tensor_scalar(DT[:, 1, :], dist, 0.0, LG[:, 1, 8 + h:9 + h], ALU.min, ALU.mult))
                        nc.vector.tensor_tensor(DT[:, 0, :], DT[:, 0, :], DT[:, 1, :], ALU.add).then_inc(rt_arg, 1)

                    v.wait_ge(at_pv[0], n_items)
                    decay_arg(0)
                    for h in range(HEADS0):
                        v.wait_ge(rt_exp, h + 1)
                        nc.vector.tensor_tensor(DC[:, h % 2, 1, :], DT[:, 2, :], DT[:, 3, :], ALU.add).then_inc(rt_dc, 1)
                        v.wait_ge(rt_dc, h + 1)
                        if h + 1 < HEADS0:
                            decay_arg(h + 1)
                        if h >= 2:
                            v.wait_ge(rt_pv, h - 1)
                        for w in range(3):
                            v.wait_ge(rt_s, 3 * h + w + 1)
                            nc.vector.tensor_tensor(ST[:, h % 2, w, :], PS[:, w, :], DC[:, h % 2, w // 2, :], ALU.mult)\
                              .then_inc(rt_m, 1)
                    v.wait_ge(rt_pv, HEADS0)
                    v.wait_ge(rt_m, 3 * HEADS0)
                    v.wait_ge(pr_sg, 1)
                    o3 = PS[:, 4:8, :].rearrange("p t (h d) -> p t h d", d=HD)
                    for t in range(NT):
                        link(nc.vector.tensor_reduce(gst[:, 0, t, :], o3[:, t], AX, ALU.add))
                    link(nc.vector.tensor_scalar(gst[:, 0, :, :], gst[:, 0, :, :], 1.0 / HD, None, ALU.mult))
                    for t in range(NT):
                        oc = OC[:, t, :].rearrange("p (h d) -> p h d", d=HD)
                        link(nc.vector.tensor_tensor(oc, o3[:, t], gst[:, 0, t, :].unsqueeze(2).broadcast_to([P, 8, HD]), ALU.subtract))
                        link(nc.vector.tensor_tensor(DT[:, 0, :], OC[:, t, :], OC[:, t, :], ALU.mult))
                        link(nc.vector.tensor_reduce(gst[:, 3, t, :], DT[:, 0, :].rearrange("p (h d) -> p h d", d=HD), AX, ALU.add))
                    nc.vector.tensor_scalar(gst[:, 1, :, :], gst[:, 3, :, :], 1.0 / HD, 1e-5, ALU.mult, ALU.add).then_inc(rt_var, 1)
                    v.wait_ge(rt_sd, 1)
                    link(nc.vector.reciprocal(gst[:, 3, :, :], gst[:, 2, :, :]))
                    for t in range(NT):
                        oc = OC[:, t, :].rearrange("p (h d) -> p h d", d=HD)
                        link(nc.vector.tensor_tensor(oc, oc, gst[:, 3, t, :].unsqueeze(2).broadcast_to([P, 8, HD]), ALU.mult))
                        nc.vector.tensor_tensor(O[:, t, 512:1024], OC[:, t, :], V0[:, 2, t, :], ALU.mult).then_inc(rt_o, 1)
                for u in range(2 * nt):
                    b, t = divmod(u, nt)
                    v.wait_ge(op_mm[l], u + 1)
                    xs = X[:, t, b * BLK:(b + 1) * BLK]
                    link(nc.vector.tensor_tensor(DT[:, u % 2, :], PS[:, 2 + u % 2, :],
                                                 rows[:, t // 2, 0, b * BLK:(b + 1) * BLK], ALU.mult))
                    nc.vector.tensor_tensor(xs, xs, DT[:, u % 2, :], ALU.add).then_inc(op_x[l], 1)
                    v.wait_ge(op_x[l], u + 1)
                for c in range(2 - l):
                    for w in range(2):
                        row_evac(rows2[:, c, w, :], n_row)
                        n_row += 1
                rms(l, 2 * l + 2, nt)
                v.wait_ge(row_ev, n_row)
                for t in range(nt):
                    link(nc.vector.scalar_tensor_tensor(out=H2[:, t, :], in0=X[:, t, :], scalar=st[:, 3, t:t + 1],
                                                        in1=rows2[:, t // 2, 0, :], op0=ALU.mult, op1=ALU.mult))
                    nc.vector.tensor_tensor(H2[:, t, :], H2[:, t, :], rows2[:, t // 2, 1, :], ALU.add).then_inc(n2_h[l], 1)
                for hp in range(16):
                    v.wait_ge(ps_mm[l], hp + 1)
                    nc.vector.tensor_copy(S[:, 0:nt, hp, :], PS[:, 2 + hp % 2, 0:nt * P].rearrange("p (t n) -> p t n", n=P))\
                      .then_inc(ps_ev[l], 1)
                v.wait_ge(ps_ev[l], 16)
                v.wait_ge(n2_h[l], nt)

                def top16(vals, idx, src, spare, lk):
                    lk(nc.vector.max(vals[:, 0:8], src), True)
                    nc.vector.max_index(idx[:, 0:8], vals[:, 0:8], src)
                    lk(nc.vector.match_replace(spare, vals[:, 0:8], src, LOWEST), True)
                    lk(nc.vector.max(vals[:, 8:16], spare), True)
                    return nc.vector.max_index(idx[:, 8:16], vals[:, 8:16], spare)

                def route(T, h, lk):
                    t = PT_[T][1]
                    lk(nc.vector.tensor_copy(rs_[:, 0:2, :], S[:, t, bass.ds(2 * h, 2), :]), True)
                    for p in range(2):
                        ins = top16(rv[:, p, :], ri[:, p, :], rs_[:, p, :], rs_[:, 2 + p, :], lk)
                    lk(ins)
                    nc.vector.tensor_copy(rf[:, 0:2, :], ri[:, 0:2, :])
                    cand = rc[:, 0, :].rearrange("p (i j) -> p i j", j=TOPK)
                    lk(nc.vector.tensor_tensor(cand, rv[:, 0, :].unsqueeze(2).broadcast_to([P, TOPK, TOPK]),
                                               rv[:, 1, :].unsqueeze(1).broadcast_to([P, TOPK, TOPK]), ALU.add), True)
                    lk(top16(rv[:, 2, :], ri[:, 2, :], rc[:, 0, :], rc[:, 1, :], lk))
                    nc.vector.tensor_single_scalar(ri[:, 3, :], ri[:, 2, :], 4, ALU.logical_shift_right)
                    lk(nc.vector.tensor_single_scalar(ri[:, 4, :], ri[:, 2, :], TOPK - 1, ALU.bitwise_and))
                    nc.vector.tensor_copy(GT[:, T % 2, bass.ds(h, 1), :], rv[:, 2:3, :])
                    lk(nc.vector.tensor_copy(rf[:, 2:4, :], ri[:, 3:5, :]))
                    for p in range(2):
                        oh = rc[:, p, :].rearrange("p (s k) -> p s k", k=TOPK)
                        lk(nc.vector.tensor_tensor(oh, rf[:, 2 + p, :].unsqueeze(2).broadcast_to([P, TOPK, TOPK]),
                                                   TB[:, T_IOTA:T_END].unsqueeze(1).broadcast_to([P, TOPK, TOPK]), ALU.is_equal))
                        lk(nc.vector.tensor_tensor(oh, oh, rf[:, p, :].unsqueeze(1).broadcast_to([P, TOPK, TOPK]), ALU.mult))
                        ins = nc.vector.tensor_reduce(rf[:, 2 + p, :], oh, AX, ALU.add)
                    lk(ins)
                    lk(nc.vector.scalar_tensor_tensor(out=ri[:, 3, :], in0=rf[:, 2, :], scalar=float(P), in1=rf[:, 3, :],
                                                      op0=ALU.mult, op1=ALU.add))
                    nc.vector.tensor_copy(IDX[:, T % 2, bass.ds(h * TOPK, TOPK)], ri[:, 3, :]).then_inc(idx_ready, 1)

                CH = 21

                def counted(base):
                    k = [0]

                    def lk(ins, apart=False):
                        k[0] += 1
                        ins.then_inc(dv, 1)
                        v.wait_ge(dv, base + k[0])
                        if apart:
                            v.sem_inc(apart_dve, 1)
                    return lk, k

                def gate_begin(T):
                    v.wait_ge(idx_ready, 8 * (T + 1))
                    nc.vector.tensor_copy(gsm[:, 0, :], GT[:, T % 2, :, 0])
                    link(nc.vector.tensor_copy(gsm[:, 1, :], GT[:, T % 2, :, 0]))
                    nc.vector.tensor_tensor(GT[:, T % 2, :, :], GT[:, T % 2, :, :],
                                            gsm[:, 0, :].unsqueeze(2).broadcast_to([P, PH, TOPK]), ALU.subtract).then_inc(gate_sub, 1)

                def gate_end(T):
                    v.wait_ge(gate_exp, T + 1)
                    link(nc.vector.tensor_reduce(gsm[:, 0, :], GT[:, T % 2, :, :], AX, ALU.add))
                    link(nc.vector.reciprocal(gsm[:, 1, :], gsm[:, 0, :]))
                    link(nc.vector.tensor_tensor(GT[:, T % 2, :, :], GT[:, T % 2, :, :],
                                                 gsm[:, 1, :].unsqueeze(2).broadcast_to([P, PH, TOPK]), ALU.mult))

                def dots(g, t, b):
                    for j in range(TOPK):
                        v.wait_ge(u_in[j % NU], g * (16 * TOPK // NU) + 16 * (j // NU + 1))
                        nc.vector.tensor_tensor_reduce(UB[:, j % NU, :], UB[:, j % NU, :], H2[:, t, :], 1.0, 0.0,
                                                       ALU.mult, ALU.add, av_[:, 0, b, j:j + 1]).then_inc(u_dot, 1)

                def weigh(g, T, h, b):
                    v.wait_ge(act_done, g + 1)
                    if not (isinstance(g, int) and g < 2):
                        v.wait_ge(dg_ready, g * TOPK - TOPK)
                    nc.vector.tensor_tensor(av_[:, 2, b, :], av_[:, 1, b, :],
                                            GT[:, T % 2, bass.ds(h, 1), :].rearrange("p a s -> p (a s)"), ALU.mult).then_inc(w_ready, 1)

                def add_tile(T):
                    t = PT_[T][1]
                    v.wait_ge(v_used, 8 * TOPK * (T + 1))
                    link(nc.vector.tensor_tensor(TMP, PS[:, 6:8, :].rearrange("p b n -> p (b n)"), rows[:, t // 2, 1, :], ALU.mult))
                    nc.vector.tensor_tensor(X[:, t, :], X[:, t, :], TMP, ALU.add).then_inc(acc_free, 1)
                    v.wait_ge(acc_free, T + 1)

                T0 = PT_.index((l, tiles[l][0]))
                base = count[0]
                with v.Fori(0, 8) as i:
                    lk, k = counted(base + i * CH)
                    route(T0, i, lk)
                    assert k[0] == CH, k[0]
                count[0] += 8 * CH
                gate_begin(T0)
                for T in range(T0, T0 + nt):
                    t = PT_[T][1]
                    nxt = T + 1 < T0 + nt
                    for h in range(2):
                        dots(8 * T + h, t, h)
                        if h == 0:
                            gate_end(T)
                        weigh(8 * T + h, T, h, h)
                        if h == 0 and T > T0:
                            add_tile(T - 1)
                        if nxt:
                            route(T + 1, h, link)
                    base = count[0] - 2 * CH
                    with v.Fori(1, 4) as i:
                        lk, k = counted(base + 2 * CH * i)
                        for e in range(2):
                            dots(8 * T + e + 2 * i, t, e)
                            weigh(8 * T + e + 2 * i, T, 2 * i + e, e)
                            if nxt:
                                route(T + 1, 2 * i + e, lk)
                    if nxt:
                        assert k[0] == 2 * CH
                        count[0] += 6 * CH
                        gate_begin(T + 1)
                add_tile(T0 + nt - 1)


_INS = ["x", "c", "ctx", "c_ctx", "mod_w", "mod_b", "norm1_g", "norm2_g", "ab_w_in", "ab_w_out", "na_q_norm",
        "na_k_norm", "ret_log_decay", "swa_w_in", "swa_w_out", "swa_q_norm", "swa_k_norm", "swa_sink",
        "peer_w_q"]


def kernel(**inputs):
    import concourse.bacc as _bacc
    from concourse.bass_utils import run_bass_kernel_spmd as _run

    nc = _bacc.Bacc("TRN2", target_bir_lowering=False, num_devices=1)
    laid = {name: np.asarray(inputs[name]) for name in _INS}
    laid["table"] = constant_table()
    rpb = np.asarray(inputs["na_rpb"])[0]
    dr, dc = bias_places()
    padded = np.concatenate([rpb, np.full(rpb.shape[:2] + (1,), NEG, rpb.dtype)], axis=2)
    laid["nab"] = padded[:, dr, dc]
    sk = np.asarray(inputs["peer_sub_keys"])
    laid["subk"] = np.ascontiguousarray(sk.transpose(0, 4, 1, 2, 3)).reshape(2, P, 16, P)
    for l in range(2):
        laid[f"peer_u{l}"] = np.asarray(inputs["peer_u"])[l]
        laid[f"peer_v{l}"] = np.asarray(inputs["peer_v"])[l]
    arrays, aps = {}, {}
    for name, arr in laid.items():
        arr = np.ascontiguousarray(arr)
        arrays[f"in_{name}"] = arr
        aps[name] = nc.dram_tensor(f"in_{name}", arr.shape, mybir.dt.from_np(arr.dtype), kind="ExternalInput").ap()
    out = nc.dram_tensor("out_0", (1, TOK, D), F32, kind="ExternalOutput").ap()
    backbone(nc, aps, out)
    r = _run(nc, [arrays], core_ids=[0])
    return r.results[0]["out_0"]
```

```python
from contextlib import ExitStack

import numpy as np

import concourse.bass as bass
from concourse import mybir

ALU = mybir.AluOpType
ACT = mybir.ActivationFunctionType
AX = mybir.AxisListType.X
F32 = mybir.dt.float32
U32 = mybir.dt.uint32

P = 128
D = 1024
KC = D // P
TOK = 256
NT = 2 * TOK // P
HD = 64
GRID_W = 64
NA_ROWS, NA_COLS = 8, 16
WINDOW = 128
NEG = -1e30
LOWEST = -3.4e38
HEADS0 = 8
HEADS1, KV1 = 16, 4
BLK = 512
NW = 3
PH = 8
TOPK = 16
NU = 8
NV = 4
NR = 4
LAG = TOPK + 4

T_ID = 0
T_ROPE = T_ID + P
T_DIST = T_ROPE + 2 * 96
T_MASK = T_DIST + 2 * TOK
T_IOTA = T_MASK + 2 * TOK
T_END = T_IOTA + TOPK


def constant_table():
    t = np.zeros((P, T_END), np.float32)
    t[:, T_ID:T_ID + P] = np.eye(P)
    tok = np.arange(TOK)
    nf = HD // 4
    inv = np.power(10000.0, -np.arange(nf) / nf)
    ang = np.concatenate([(tok // GRID_W)[:, None] * inv, (tok % GRID_W)[:, None] * inv], axis=1)
    rope = np.concatenate([np.cos(ang), -np.sin(ang), np.sin(ang)], axis=1)
    t[:, T_ROPE:T_DIST] = rope.reshape(2, P, 96).transpose(1, 0, 2).reshape(P, 192)
    i, j = np.arange(TOK)[None, :], np.arange(TOK)[:, None]
    t[:, T_DIST:T_MASK] = (i - j).reshape(2, P, TOK).transpose(1, 0, 2).reshape(P, 2 * TOK)
    out = np.abs(i - j) > WINDOW
    t[:, T_MASK:T_IOTA] = np.where(out, NEG, 0.0).reshape(2, P, TOK).transpose(1, 0, 2).reshape(P, 2 * TOK)
    t[:, T_IOTA:] = np.arange(TOPK)
    return t


def bias_places():
    rows = TOK // GRID_W
    kr = min(NA_ROWS, rows)
    t = np.arange(TOK)
    r, c = t // GRID_W, t % GRID_W
    r0 = np.clip(r - kr // 2, 0, rows - kr)
    c0 = np.clip(c - NA_COLS // 2, 0, GRID_W - NA_COLS)
    dr = r[None, :] - r[:, None] + NA_ROWS - 1
    dc = c[None, :] - c[:, None] + NA_COLS - 1
    inside = ((r[None] >= r0[:, None]) & (r[None] < r0[:, None] + kr)
              & (c[None] >= c0[:, None]) & (c[None] < c0[:, None] + NA_COLS))
    return dr, np.where(inside, dc, 2 * NA_COLS - 1)


def spread(costs, first, last):
    total, at, out = sum(costs), 0.0, []
    for c in costs:
        out.append(first + int(at / total * (last - first)))
        at += c
    return out


def backbone(nc, a, out):
    with ExitStack() as ctx:
        def sb(name, shape, dt=F32):
            return ctx.enter_context(nc.sbuf_tensor(name, shape, dt))

        def sem(name):
            return ctx.enter_context(nc.semaphore(name))

        PASS = [(0, [2, 3]), (0, [0, 1]), (1, [0]), (1, [1])]
        NORM = [(0, [2, 3]), (0, [0, 1]), (1, [2, 3]), (1, [0]), (1, [1])]
        KIND0 = ["q", "k", "v", "rq", "rk", "rv", "gate"]
        UNITS, U_OF = [], []
        for l, tl in NORM:
            a0 = len(UNITS)
            if l == 0:
                UNITS += [(0, g, t, k) for g, k in enumerate(KIND0) for t in tl]
            else:
                UNITS += [(1, 2, t, "kv") for t in tl]
                if tl[0] < 2:
                    UNITS += [(1, g, t, "q") for g in range(2) for t in tl]
            U_OF.append((a0, len(UNITS)))
        NORMED, TURNED = ("q", "k", "kv"), ("q", "k", "kv", "rq", "rk")
        normed = [sum(u[3] in NORMED for u in UNITS[:n]) for n in range(len(UNITS) + 1)]
        turned = [sum(u[3] in TURNED for u in UNITS[:n]) for n in range(len(UNITS) + 1)]
        ITEMS, I_OF = [], []
        for l, tl in PASS:
            a0 = len(ITEMS)
            ITEMS += [(l, h, t) for h in range((HEADS0, HEADS1)[l]) for t in tl]
            I_OF.append((a0, len(ITEMS)))
        XN_OF = np.cumsum([0] + [len(tl) for _, tl in NORM]).tolist()
        T_OF = np.cumsum([0] + [len(tl) for _, tl in PASS]).tolist()
        TILE = [(l, t) for l, tl in PASS for t in tl]
        RET = [0, HEADS0, 3 * HEADS0]
        RMS = {k: n for n, k in enumerate([("n1", 0), ("n2", 0), ("n1", 1), ("n2", 1), ("n1", 2), ("n1", 3),
                                           ("n1", 4), ("n2", 2), ("n2", 3)])}
        ROW = {k: n for n, k in enumerate([(p, w) for p in range(4) for w in ("g1", "g2", "A2", "sh2")
                                           if (p, w) != (3, "g2")])}
        VEC = {"g1": 2, "sh2": 3, "A2": 4, "g2": 5}

        X = sb("resid", [P, NT, D])
        W = sb("wring", [P, NW, 2048])
        G2 = sb("g2_rows", [P, 2, D])
        TB = sb("table", [P, T_END])
        VC = sb("vec_cols", [P, P])
        MC = [sb(f"mod_cols{l}", [P, 48, 2]) for l in range(2)]
        SC = sb("silu_c", [P, 2, KC])
        gains = sb("gains", [P, 4, HD])
        LG = sb("log_gamma", [P, 4, 16])
        sink = sb("sink", [P, 2, HEADS1])
        st = sb("stats", [P, 4, NT])
        sums = sb("sums", [P, 5, len(ITEMS)])
        gst = sb("gn_stats", [P, 4, 2, 8])
        nst = sb("unit_stats", [P, 2, 3, 8])
        TOPV = sb("top_vals", [P, 3, 16, TOPK])
        TOPI = sb("top_idx", [P, 3, 16, TOPK], U32)
        spare = sb("spare", [P, 2, P])
        IDX = sb("idx", [P, NR, TOPK], U32)
        BEST = sb("best", [P, NR, TOPK])
        EXPS = sb("exps", [P, NR, TOPK])
        EZ = sb("exp_sum", [P, 3, NR])
        ri = sb("route_idx", [P, 3, TOPK], U32)
        rf = sb("route_idx_f", [P, 4, TOPK])
        rc = sb("route_cand", [P, 2, TOPK * TOPK])
        av_ = sb("act_w", [P, 3, 2, TOPK])
        diag = sb("diag", [P, NV, P])
        TMP = sb("tmp", [P, 512])
        UB = sb("u_rows", [P, NU, D])
        VB = sb("v_rows", [P, NV, D])
        H2 = sb("h2", [P, 3, D])
        AR = sb("arena", [P, 18432])
        PS = ctx.enter_context(nc.psum_tensor("ps", [P, 8, 512], F32))
        ident = TB[:, T_ID:T_ID + P]

        def view(a0, n, pattern, **k):
            return AR[:, a0:a0 + n].rearrange(pattern, **k)

        QA = view(0, 2048, "p (w c n) -> p w c n", w=2, c=4)
        KA = view(2048, 4096, "p (w c n) -> p w c n", w=2, c=4)
        VA = view(6144, 4096, "p (w t n) -> p w t n", w=2, t=NT)
        SK = view(0, 2048, "p (h n) -> p h n", h=16)
        K1T = view(2048, 2048, "p (c n) -> p c n", c=4)
        V1 = view(4096, 1024, "p (t n) -> p t n", t=NT)
        Q1T = view(6144, 2048, "p (t c n) -> p t c n", t=2, c=8)
        O = view(10240, 2048, "p (t n) -> p t n", t=2)
        XN = O
        HT = view(12288, 2048, "p (k n) -> p k n", k=KC)
        M0 = 14336
        SQ = view(M0, 1024, "p (b n) -> p b n", b=2)
        QN = view(M0 + 1024, 1024, "p (b n) -> p b n", b=2)
        T1, T2 = AR[:, M0 + 2048:M0 + 2560], AR[:, M0 + 2560:M0 + 3072]
        PB = view(M0, 1024, "p (b n) -> p b n", b=2)
        PT = view(M0 + 1024, 1024, "p (b k n) -> p b k n", b=2, k=4)
        NB = view(M0 + 3072, 1024, "p (b t n) -> p b t n", b=2, t=2)
        ST = view(M0, 2048, "p (b w n) -> p b w n", b=2, w=2)
        DC = view(M0 + 2048, 1024, "p (w n) -> p w n", w=2)
        DT = view(M0 + 3072, 1024, "p (w n) -> p w n", w=2)
        OC = view(M0, 1024, "p (t n) -> p t n", t=2)
        G1 = AR[:, M0:M0 + 1024]
        YT = view(M0 + 1024, 1024, "p (b n) -> p b n", b=2)
        ROWS2 = view(M0 + 2048, 2048, "p (w n) -> p w n", w=2)

        def MR(l, b):
            return VB[0:2, b % 2, 0:512] if l == 0 else AR[0:2, M0 + 2048 + 512 * (b % 2):M0 + 2560 + 512 * (b % 2)]

        def MP(l, b):
            return PS[0:2, 6 if l == 0 and b >= 4 else b % 2, :]

        def MT(l):
            return PS[:, 7 if l == 0 else 5, :]

        QTB = view(M0, 512, "p (b n) -> p b n", b=2)

        ld_tab, ld_x, ld_row, ld_g = sem("ld_tab"), sem("ld_x"), sem("ld_row"), sem("ld_g")
        setup_t, setup_sc, dv = sem("setup_t"), sem("setup_sc"), sem("dve_chain")
        lg_e, lg_done = sem("lg_e"), sem("lg_done")
        w_in = [sem(f"w_in{i}") for i in range(NW)]
        mod_mm, mod_row, mod_tr, mc_done = sem("mod_mm"), sem("mod_row"), sem("mod_tr"), sem("mc_done")
        row_mm, row_ev = sem("row_mm"), sem("row_ev")
        n_ms, n_rt, n_rs = sem("n_ms"), sem("n_rt"), sem("n_rs")
        n1_xn, n1_tr, n1_ev = sem("n1_xn"), sem("n1_tr"), sem("n1_ev")
        pr_half, pr_mm, pr_free, pr_sq, pr_ms = sem("pr_half"), sem("pr_mm"), sem("pr_free"), sem("pr_sq"), sem("pr_ms")
        pr_rt, pr_qn, pr_tr, pr_ev, pr_gate = sem("pr_rt"), sem("pr_qn"), sem("pr_tr"), sem("pr_ev"), sem("pr_gate")
        at_s, at_max, at_exp, at_tr = sem("at_s"), sem("at_max"), sem("at_exp"), sem("at_tr")
        at_pT, at_pv, at_o = sem("at_pT"), sem("at_pv"), sem("at_o")
        nb_in = [sem(f"nb_in{i}") for i in range(2)]
        rt_arg, rt_exp, rt_dc, rt_s = sem("rt_arg"), sem("rt_exp"), sem("rt_dc"), sem("rt_s")
        rt_m, rt_pv, rt_var, rt_sd, rt_o = sem("rt_m"), sem("rt_pv"), sem("rt_var"), sem("rt_sd"), sem("rt_o")
        op_tr, op_ev, op_half, op_mm, op_x = sem("op_tr"), sem("op_ev"), sem("op_half"), sem("op_mm"), sem("op_x")
        sk_in, n2_h, n2_tr, n2_ev = sem("sk_in"), sem("n2_h"), sem("n2_tr"), sem("n2_ev")
        pq_mm, pq_ev, ps_mm, tp_done = sem("pq_mm"), sem("pq_ev"), sem("ps_mm"), sem("tp_done")
        routed, exps_done = sem("routed"), sem("exps_done")
        u_in = [sem(f"u_in{i}") for i in range(NU)]
        v_in = [sem(f"v_in{i}") for i in range(NV)]
        u_dot, act_done, w_ready = sem("u_dot"), sem("gelu_done"), sem("w_ready")
        dg_ready, v_used, tile_added, st_out = sem("diag_ready"), sem("v_used"), sem("tile_added"), sem("st_out")

        blocks = []

        def group(kind, l, n, b, split, freed):
            for half in range(2):
                blocks.append(((kind, n, b, half), kind, l, b, split, half, freed[half]))

        for n in range(4):
            group("mod", 0, 0, n, "C", [(mod_mm, 2 * n + 1), (mod_mm, 2 * n + 2)])

        def in_groups(j):
            u0, u1 = U_OF[j]
            for g in dict.fromkeys(UNITS[u][1] for u in range(u0, u1)):
                last = max(u for u in range(u0, u1) if UNITS[u][1] == g)
                group("in", NORM[j][0], j, g, "K", [(pr_half, last + 1), (pr_mm, last + 1)])

        def out_groups(p):
            nt, o0 = len(PASS[p][1]), 2 * T_OF[p]
            for b in range(2):
                group("out", PASS[p][0], p, b, "K", [(op_half, o0 + nt * (b + 1)), (op_mm, o0 + nt * (b + 1))])
            for b in range(4):
                group("wq", PASS[p][0], p, b, "C", [(pq_mm, 16 * p + 4 * b + 2), (pq_mm, 16 * p + 4 * b + 4)])

        in_groups(0)
        for n in range(4, 12):
            group("mod", 0, 0, n, "C", [(mod_mm, 2 * n + 1), (mod_mm, 2 * n + 2)])
        out_groups(0)
        in_groups(1)
        out_groups(1)
        for n in range(12):
            group("mod", 1, 1, n, "C", [(mod_mm, 24 + 2 * n + 1), (mod_mm, 24 + 2 * n + 2)])
        for j in (2, 3, 4):
            in_groups(j)
        out_groups(2)
        out_groups(3)
        place = {b[0]: n for n, b in enumerate(blocks)}

        def w_wait(eng, key):
            n = place[key]
            eng.wait_ge(w_in[n % NW], 16 * (n // NW + 1))
            return W[:, n % NW, :]

        def c_norm(j):
            return [2.0] + [0.5 * len(NORM[j][1])] * 4

        def c_proj(j):
            u0, u1 = U_OF[j]
            return [7.2] * (u1 - u0) + [0.5] * 2

        def c_attn(p):
            i0, i1 = I_OF[p]
            return [2.9] * (i1 - i0) + [1.0] * 2

        def c_ret(p):
            return [4.0] * (HEADS0 + 1) + [2.0]

        def c_out(p):
            nt = len(PASS[p][1])
            return [1.8] + [0.5] * (2 * nt) + [6.8] * (2 * nt)

        def c_prep(p):
            nt = len(PASS[p][1])
            return [1.8] * 3 + [2.5] + [0.5] * (2 * nt) + [1.95 * nt] * 16 + [0.5]

        def table_of(*parts):
            out = {}
            for costs, first, last in parts:
                for s in spread(costs, first, last):
                    out[s] = out.get(s, 0) + 1
            return out

        S1 = TOPK * 8
        c1 = c_norm(1) + c_proj(1) + c_attn(1) + c_ret(1) + c_out(1) + c_prep(1)
        c3 = c_attn(3) + c_out(3) + c_prep(3)
        WINDOWS = [(0, 4), (4, 6)]
        READY = [3 + 1 + 2 * len(tl) + 5 for _, tl in PASS]
        BESIDE = {0: table_of((c_prep(0)[READY[0]:], 1, 19), (c1, 19, 14 * TOPK + 8),
                              ([3.4] * 24 + [1.0], 2 * S1, 3 * S1), (c_norm(2) + c_proj(2), 3 * S1, 3 * S1 + 24),
                              (c_norm(3) + c_proj(3), 3 * S1 + 26, 4 * S1 - 10)),
                  4: table_of((c_prep(2)[READY[2]:], 4 * S1 + 1, 4 * S1 + 13), (c3, 4 * S1 + 13, 4 * S1 + 6 * TOPK + 8))}

        def chain(*steps):
            for s in steps:
                yield from s

        def beside(main, other):
            for _ in main:
                next(other, None)
                yield
            for _ in other:
                yield

        def ready(p, steps):
            for _ in range(READY[p]):
                next(steps)
            return steps

        def steps_at(T0, slot, steps):
            for _ in range(BESIDE[T0].get(slot, 0)):
                next(steps)

        block = ctx.enter_context(nc.Block())

        @block.sync
        def _(sp):
            sp.dma_start(TB[:, :], a["table"]).then_inc(ld_tab, 16)
            sm = W[:, 2, :]
            sp.dma_start(sm[0:96, 0:P], a["mod_b"].rearrange("l (j p) -> (l j) p", p=P)).then_inc(ld_row, 16)
            sp.dma_start(sm[96:112, 0:P], a["norm1_g"].rearrange("l (j p) -> (l j) p", p=P)).then_inc(ld_row, 16)
            sp.dma_start(sm[112:128, 0:P], a["norm2_g"].rearrange("l (j p) -> (l j) p", p=P)).then_inc(ld_row, 16)
            sp.dma_start(sm[0:8, P:2 * P], a["c"].rearrange("b (j p) -> (b j) p", p=P)).then_inc(ld_row, 16)
            sp.dma_start(sm[8:16, P:2 * P], a["c_ctx"].rearrange("(j p) -> j p", p=P)).then_inc(ld_row, 16)
            src = {"mod": lambda l: a["mod_w"][l], "in": lambda l: (a["ab_w_in"], a["swa_w_in"])[l][0],
                   "out": lambda l: (a["ab_w_out"], a["swa_w_out"])[l][0], "wq": lambda l: a["peer_w_q"][l]}
            for n, (_, kind, l, b, split, half, _) in enumerate(blocks):
                if n == 2:
                    sp.wait_ge(setup_t, 2)
                if n >= NW:
                    sp.wait_ge(*blocks[n - NW][6])
                w = src[kind](l)
                if split == "K":
                    w = w[half * 512:(half + 1) * 512, b * BLK:(b + 1) * BLK]
                else:
                    w = w[:, b * BLK + half * 256:b * BLK + (half + 1) * 256]
                cols = 512 if split == "K" else 256
                sp.dma_start(W[:, n % NW, :].rearrange("p (k n) -> p k n", n=cols),
                             w.rearrange("(k p) n -> p k n", p=P)).then_inc(w_in[n % NW], 16)
            sp.wait_ge(tile_added, len(TILE))
            sp.dma_start(out.rearrange("b (t p) d -> p (b t) d", p=P), X[:, 0:2, :]).then_inc(st_out, 16)
            sp.wait_ge(st_out, 16)

        @block.gpsimd
        def _(pool):
            def gather(table, g, j, ring, nring, landed):
                nc.gpsimd.indirect_dma_start(
                    out=ring[:, j % nring, :], out_offset=None, in_=table,
                    in_offset=bass.IndirectOffsetOnAxis(ap=IDX[:, g % NR, j:j + 1], axis=0))\
                    .then_inc(landed[j % nring], 16)

            for T0, T1_ in WINDOWS:
                l = TILE[T0][0]
                for slot in range(S1 * T0, S1 * T1_ + LAG):
                    if slot < S1 * T1_:
                        if slot % TOPK == 0:
                            pool.wait_ge(routed, slot // TOPK + 1)
                        if slot >= NU:
                            pool.wait_ge(u_dot, slot - NU + 1)
                        gather(a[f"peer_u{l}"], slot // TOPK, slot % TOPK, UB, NU, u_in)
                    s = slot - LAG
                    if s >= S1 * T0:
                        if s >= NV:
                            pool.wait_ge(v_used, s - NV + 1)
                        gather(a[f"peer_v{l}"], s // TOPK, s % TOPK, VB, NV, v_in)

        @block.tensor
        def _(pe):
            def turn(dst, src, n=P):
                return nc.tensor.transpose(dst, src, ident[0:n, 0:n])

            def ada(l, blocks_of_ada):
                for b in blocks_of_ada:
                    if l == 0 and b >= 5:
                        pe.wait_ge(mod_row, b)
                    for half in range(2):
                        w = w_wait(pe, ("mod", l, b, half)).rearrange("p (k n) -> p k n", n=256)
                        for k in range(KC):
                            mm = nc.tensor.matmul(MP(l, b)[:, half * 256:(half + 1) * 256], SC[:, :, k], w[:, k, :],
                                                  start=k == 0, stop=k == KC - 1)
                        mm.then_inc(mod_mm, 1)
                        if half == 0 and b > blocks_of_ada[0]:
                            mod_turn(l, b - 1)
                        yield
                mod_turn(l, blocks_of_ada[-1])
                yield

            def mod_turn(l, b):
                if l == 1 and b == 0:
                    pe.wait_ge(row_ev, ROW[1, "sh2"] + 1)
                pe.wait_ge(mod_row, 12 * l + b + 1)
                for jj in range(4):
                    j = 4 * b + jj
                    mm = turn(MT(l)[:, 2 * j:2 * j + 2], MR(l, b)[:, jj * P:(jj + 1) * P], 2)
                mm.then_inc(mod_tr, 1)

            def row(p, which):
                l, tl = PASS[p]
                c, v, n = tl[0] // 2, VEC[which], ROW[p, which]
                pe.wait_ge(mc_done, l + 2)
                if n:
                    pe.wait_ge(row_ev, n)
                for k in range(KC):
                    mm = nc.tensor.matmul(PS[:, 4 + k // 4, (k % 4) * P:(k % 4 + 1) * P],
                                          MC[l][:, v * KC + k, c:c + 1].broadcast_to([P, P]), ident, start=True, stop=True)
                mm.then_inc(row_mm, 1)

            def norm1(j):
                yield
                tl = NORM[j][1]
                nt = len(tl)
                pe.wait_ge(n1_xn, XN_OF[j + 1])
                pe.wait_ge(*[(mc_done, 1), (tp_done, 16), (tp_done, 32), (pr_ev, turned[U_OF[2][1]]),
                             (pr_ev, turned[U_OF[3][1]])][j])
                for m in range(4):
                    u = 4 * j + m
                    if m >= 2:
                        pe.wait_ge(n1_ev, u - 1)
                    for kk in range(2):
                        for e in range(nt):
                            mm = turn(PS[:, 2 + m % 2, (kk * nt + e) * P:(kk * nt + e + 1) * P],
                                      XN[:, tl[e] % 2, (2 * m + kk) * P:(2 * m + kk + 1) * P])
                    mm.then_inc(n1_tr, 1)
                    yield

            def proj(j):
                u0, u1 = U_OF[j]
                pe.wait_ge(n1_ev, 4 * j + 4)
                if j:
                    pe.wait_ge(pq_ev, 16 * min(j, 2))
                    pe.wait_ge(row_ev, ROW[min(j, 2) - 1, "sh2"] + 1)
                for u in range(u0, u1 + 2):
                    if u < u1:
                        l, g, t, kind = UNITS[u]
                        if u >= 3:
                            pe.wait_ge(pr_free, u - 2)
                        for half in range(2):
                            w = w_wait(pe, ("in", j, g, half)).rearrange("p (k n) -> p k n", n=512)
                            for k in range(4):
                                mm = nc.tensor.matmul(PS[:, (0, 1, 4)[u % 3], :], HT[:, 4 * half + k, (t % 2) * P:(t % 2 + 1) * P],
                                                      w[:, k, :], start=half + k == 0, stop=half + k == 4)
                            mm.then_inc((pr_half, pr_mm)[half], 1)
                    m = u - 2
                    if m >= u0 and UNITS[m][3] in TURNED:
                        n = turned[m]
                        pe.wait_ge(pr_qn, n + 1)
                        if n >= 2:
                            pe.wait_ge(pr_ev, n - 1)
                        for c in range(4):
                            mm = turn(PS[:, 2 + n % 2, c * P:(c + 1) * P], QN[:, n % 2, c * P:(c + 1) * P])
                        mm.then_inc(pr_tr, 1)
                    yield

            def keep_busy(p):
                if p == 2:
                    nc.tensor.matmul(PS[:, 6, 0:TOK], ident, TB[:, T_MASK:T_MASK + TOK], start=True, stop=True)

            def attn(p):
                i0, i1 = I_OF[p]
                j = [0, 1, 4, 4][p]
                pe.wait_ge(pr_ev, turned[U_OF[j][1]])
                pe.wait_ge(pr_free, U_OF[j][1])
                if p == 2:
                    pe.wait_ge(tile_added, 4)
                if p == 3:
                    pe.wait_ge(tp_done, 48)
                    pe.wait_ge(pq_ev, 48)
                    pe.wait_ge(row_ev, ROW[2, "sh2"] + 1)
                for i in range(i0, i1 + 2):
                    if i < i1:
                        l, h, t = ITEMS[i]
                        lo = HD * (h % 2)
                        if l == 0:
                            q, k = QA[lo:lo + HD, 0, h // 2, (t % 2) * P:(t % 2 + 1) * P], KA[lo:lo + HD, 0, h // 2, :]
                            bias = None
                            if t < 2:
                                pe.wait_ge(nb_in[h % 2], 16 * (h // 2 + 1))
                                bias = NB[:, h % 2, t, :]
                        else:
                            q, k = Q1T[lo:lo + HD, t, h // 2, :], K1T[lo:lo + HD, h // 4, :]
                            bias = TB[:, T_MASK + t * TOK:T_MASK + (t + 1) * TOK]
                        if i >= 2:
                            pe.wait_ge(at_exp, i - 1)
                        if bias is None:
                            mm = nc.tensor.matmul(PS[:, i % 2, 0:TOK], q, k[:, TOK:], start=True, stop=True)
                        else:
                            nc.tensor.matmul(PS[:, i % 2, 0:TOK], ident, bias, start=True, stop=False)
                            nc.tensor.matmul(PS[:, i % 2, 0:TOK], q, k[:, 0:TOK], start=False, stop=True)
                            mm = nc.tensor.matmul(PS[:, i % 2, TOK:2 * TOK], q, k[:, TOK:2 * TOK], start=True, stop=True)
                        mm.then_inc(at_s, 1)
                    keep_busy(p)
                    if i0 <= i - 1 < i1:
                        m = i - 1
                        pe.wait_ge(at_exp, m + 1)
                        if m >= 2:
                            pe.wait_ge(at_pT, m - 1)
                        for c in range(4 if ITEMS[m][2] < 2 else 2):
                            mm = turn(PS[:, 2 + m % 2, c * P:(c + 1) * P], PB[:, m % 2, c * P:(c + 1) * P])
                        mm.then_inc(at_tr, 1)
                    if i - 2 >= i0:
                        m = i - 2
                        l, h, t = ITEMS[m]
                        kts = [0, 1, 2, 3] if t < 2 else [2, 3]
                        pe.wait_ge(at_pT, m + 1)
                        if m >= 2:
                            pe.wait_ge(at_o, m - 1)
                        for c, kt in enumerate(kts):
                            val = VA[:, 0, kt, h * HD:(h + 1) * HD] if l == 0 else V1[:, kt, (h // 4) * HD:(h // 4 + 1) * HD]
                            mm = nc.tensor.matmul(PS[:, 4 + m % 2, 0:HD], PT[:, m % 2, c, :], val,
                                                  start=c == 0, stop=c == len(kts) - 1)
                        mm.then_inc(at_pv, 1)
                    yield

            def ret(p):
                per = p + 1
                pe.wait_ge(at_o, I_OF[p][1])
                pe.wait_ge(at_exp, I_OF[p][1])
                for h in range(HEADS0 + 1):
                    if h < HEADS0:
                        lo = HD * (h % 2)
                        for w in range(per):
                            n = RET[p] + per * h + w
                            if h >= 2:
                                pe.wait_ge(rt_m, n - 2 * per + 1)
                            k0 = 2 if (p == 0 or w == 1) else 0
                            for e in range(2):
                                mm = nc.tensor.matmul(PS[:, 2 * (h % 2) + w, e * TOK:(e + 1) * TOK],
                                                      KA[lo:lo + HD, 1, h // 2, (k0 + e) * P:(k0 + e + 1) * P],
                                                      QA[lo:lo + HD, 1, h // 2, :], start=True, stop=True)
                            mm.then_inc(rt_s, 1)
                    if h >= 1:
                        m = h - 1
                        pe.wait_ge(rt_m, RET[p] + per * h)
                        for t in range(2):
                            todo = [(w, e, (2 if (p == 0 or w == 1) else 0) + e) for w in range(per) for e in range(2)]
                            for n, (w, e, kt) in enumerate(todo):
                                mm = nc.tensor.matmul(PS[:, 4 + t, m * HD:(m + 1) * HD],
                                                      ST[:, m % 2, w, e * TOK + t * P:e * TOK + t * P + P],
                                                      VA[:, 1, kt, m * HD:(m + 1) * HD], start=n == 0, stop=n == len(todo) - 1)
                        mm.then_inc(rt_pv, 1)
                    yield
                yield

            def outp(p):
                l, tl = PASS[p]
                nt, t0 = len(tl), T_OF[p]
                if l == 0:
                    pe.wait_ge(rt_o, 2 * p + 2)
                pe.wait_ge(at_o, I_OF[p][1])
                row(p, "g1")
                yield
                for n in range(2 * nt):
                    t, q = tl[n // 2], n % 2
                    if n >= 2:
                        pe.wait_ge(op_ev, 2 * t0 + n - 1)
                    for c in range(4):
                        mm = turn(PS[:, 2 + n % 2, c * P:(c + 1) * P], O[:, t % 2, (4 * q + c) * P:(4 * q + c + 1) * P])
                    mm.then_inc(op_tr, 1)
                    yield
                pe.wait_ge(op_ev, 2 * (t0 + nt))
                for u in range(2 * nt):
                    b, t = u // nt, tl[u % nt]
                    if u >= 2:
                        pe.wait_ge(op_x, 2 * t0 + u - 1)
                    for half in range(2):
                        w = w_wait(pe, ("out", p, b, half)).rearrange("p (k n) -> p k n", n=512)
                        for k in range(4):
                            mm = nc.tensor.matmul(PS[:, u % 2, :], HT[:, 4 * half + k, (t % 2) * P:(t % 2 + 1) * P], w[:, k, :],
                                                  start=half + k == 0, stop=half + k == 4)
                        mm.then_inc((op_half, op_mm)[half], 1)
                    yield

            def prep(p):
                l, tl = PASS[p]
                nt, t0 = len(tl), T_OF[p]
                for which in ("g2", "A2", "sh2"):
                    if (p, which) in ROW:
                        row(p, which)
                    yield
                yield
                pe.wait_ge(op_x, 2 * (t0 + nt))
                for n in range(2 * nt):
                    t, q = t0 + n // 2, n % 2
                    pe.wait_ge(n2_h, t + 1)
                    if n >= 2:
                        pe.wait_ge(n2_ev, 2 * t0 + n - 1)
                    for c in range(4):
                        mm = turn(PS[:, 2 + n % 2, c * P:(c + 1) * P], H2[:, t % 3, (4 * q + c) * P:(4 * q + c + 1) * P])
                    mm.then_inc(n2_tr, 1)
                    yield
                pe.wait_ge(n2_ev, 2 * (t0 + nt))
                pe.wait_ge(sk_in, 16 * min(p + 1, 3))
                lo = (tl[0] % 2) * P
                for hp in range(17):
                    if hp < 16:
                        n = 16 * p + hp
                        w = w_wait(pe, ("wq", p, hp // 4, hp % 4 // 2)).rearrange("p (k n) -> p k n", n=256)
                        if hp >= 2:
                            pe.wait_ge(pq_ev, n - 1)
                        for k in range(KC):
                            mm = nc.tensor.matmul(PS[:, hp % 2, 0:nt * P], w[:, k, (hp % 2) * P:(hp % 2 + 1) * P],
                                                  HT[:, k, lo:lo + nt * P], start=k == 0, stop=k == KC - 1)
                        mm.then_inc(pq_mm, 1)
                    if hp >= 1:
                        m = hp - 1
                        pe.wait_ge(pq_ev, 16 * p + m + 1)
                        if m >= 2:
                            pe.wait_ge(tp_done, 16 * p + m - 1)
                        for e in range(nt):
                            mm = nc.tensor.matmul(PS[:, 2 + m % 2, e * P:(e + 1) * P], QTB[:, m % 2, e * P:(e + 1) * P],
                                                  SK[:, m, :], start=True, stop=True)
                        mm.then_inc(ps_mm, 1)
                    yield

            def gathers(T0, T1_, steps):
                for slot in range(S1 * T0, S1 * T1_ + LAG):
                    steps_at(T0, slot, steps)
                    s = slot - LAG
                    if s < S1 * T0:
                        continue
                    if s % S1 == 0 and s:
                        pe.wait_ge(tile_added, s // S1)
                    j = s % TOPK
                    pe.wait_ge(v_in[j % NV], 16 * (s // NV + 1))
                    pe.wait_ge(dg_ready, s + 1)
                    for e in range(2):
                        mm = nc.tensor.matmul(PS[:, 6 + e, :], diag[:, j % NV, :], VB[:, j % NV, e * 512:(e + 1) * 512],
                                              start=s % S1 == 0, stop=s % S1 == S1 - 1, skip_group_check=True)
                    mm.then_inc(v_used, 1)
                assert next(steps, "end") == "end"

            pe.wait_ge(ld_tab, 16)
            pe.wait_ge(ld_row, 80)
            turn(PS[:, 6, 0:P], W[:, 2, 0:P]).then_inc(setup_t, 1)
            turn(PS[:, 7, 0:16], W[0:16, 2, P:2 * P], 16).then_inc(setup_t, 1)
            pe.wait_ge(setup_sc, 1)
            for _ in chain(ada(0, range(4)), norm1(0), proj(0), beside(chain(attn(0), ret(0)), ada(0, range(4, 12))), outp(0)):
                pass
            rest = ready(0, prep(0))
            gathers(0, 4, chain(rest, norm1(1), proj(1), attn(1), ret(1), outp(1), prep(1),
                                ada(1, range(12)), norm1(2), proj(2), norm1(3), proj(3)))
            for _ in chain(norm1(4), proj(4), attn(2), outp(2)):
                pass
            rest = ready(2, prep(2))
            gathers(4, 6, chain(rest, attn(3), outp(3), prep(3)))

        @block.scalar
        def _(act):
            def load_bias(h):
                act.dma_start(NB[:, h % 2, :, :], a["nab"][h].rearrange("(t p) n -> p t n", p=P)).then_inc(nb_in[h % 2], 16)

            def root(which, n, tl):
                act.wait_ge(n_ms, RMS[which, n] + 1)
                lo, hi = tl[0], tl[-1] + 1
                nc.scalar.activation(st[:, 2, lo:hi], st[:, 1, lo:hi], ACT.Sqrt).then_inc(n_rt, 1)

            def ada(l, bs):
                for b in bs:
                    yield
                    act.wait_ge(mod_mm, 24 * l + 2 * b + 2)
                    if b >= 2:
                        act.wait_ge(mod_tr, 12 * l + b - 1)
                    nc.scalar.activation(MR(l, b), MP(l, b), ACT.Copy).then_inc(mod_row, 1)
                    yield
                yield

            def norm1(j):
                l, tl = NORM[j]
                root("n1", j, tl)
                act.wait_ge(n_rs, RMS["n1", j] + 1)
                for t in tl:
                    nc.scalar.activation(XN[:, t % 2, :], X[:, t, :], ACT.Copy, scale=st[:, 3, t:t + 1]).then_inc(n1_xn, 1)
                yield
                for m in range(4):
                    yield

            def proj(j):
                u0, u1 = U_OF[j]
                for u in range(u0, u1 + 2):
                    if u < u1 and UNITS[u][3] in NORMED:
                        n = normed[u]
                        wd = 256 if UNITS[u][3] == "kv" else 512
                        act.wait_ge(pr_mm, u + 1)
                        if n >= 2:
                            act.wait_ge(pr_ms, n - 1)
                        if UNITS[u][0] == 1 and turned[u] >= 2:
                            act.wait_ge(pr_qn, turned[u] - 1)
                        nc.scalar.activation(SQ[:, n % 2, 0:wd], PS[:, (0, 1, 4)[u % 3], 0:wd], ACT.Square).then_inc(pr_sq, 1)
                    m = u - 1
                    if u0 <= m < u1 and UNITS[m][3] in NORMED:
                        n = normed[m]
                        act.wait_ge(pr_ms, n + 1)
                        nc.scalar.activation(nst[:, n % 2, 1, :], nst[:, n % 2, 0, :], ACT.Sqrt).then_inc(pr_rt, 1)
                    m = u - 2
                    if m >= u0 and UNITS[m][3] in TURNED:
                        l, g, t, kind = UNITS[m]
                        n = turned[m]
                        act.wait_ge(pr_tr, n + 1)
                        e = t % 2
                        if l == 0:
                            dst = (QA[:, int(kind == "rq"), :, e * P:(e + 1) * P] if kind in ("q", "rq")
                                   else KA[:, int(kind == "rk"), :, t * P:(t + 1) * P])
                        else:
                            dst = Q1T[:, t, 4 * g:4 * g + 4, :] if kind == "q" else K1T[:, :, t * P:(t + 1) * P]
                        nc.scalar.activation(dst, PS[:, 2 + n % 2, :].rearrange("p (c n) -> p c n", c=4), ACT.Copy,
                                             scale=HD ** -0.5 if kind in ("q", "rq") else 1.0).then_inc(pr_ev, 1)
                    yield

            def attn(p):
                i0, i1 = I_OF[p]
                l = PASS[p][0]
                j = [0, 1, 4, 4][p]
                act.wait_ge(pr_free, U_OF[j][1])
                act.wait_ge(pr_ms, normed[U_OF[j][1]])
                if l == 0:
                    nc.scalar.activation(O[:, :, 512:1024], O[:, :, 512:1024], ACT.Silu).then_inc(pr_gate, 1)
                if p == 1:
                    act.wait_ge(pr_qn, turned[U_OF[j][1]])
                    load_bias(0)
                    load_bias(1)
                for i in range(i0, i1 + 2):
                    if i < i1:
                        _, h, t = ITEMS[i]
                        nk = TOK if t >= 2 else 2 * TOK
                        act.wait_ge(at_max, i + 1)
                        if i - 2 >= i0:
                            act.wait_ge(at_tr, i - 1)
                        if p == 1 and t == 0 and 1 <= h < HEADS0 - 1:
                            load_bias(h + 1)
                        if l == 1:
                            nc.scalar.activation(sums[:, 2, i:i + 1], sink[:, 0, h:h + 1], ACT.Exp, bias=sums[:, 1, i:i + 1])
                        nc.scalar.activation(PB[:, i % 2, 0:nk], PS[:, i % 2, 0:nk], ACT.Exp, bias=sums[:, 1, i:i + 1],
                                             accum_out=sums[:, 0, i:i + 1]).then_inc(at_exp, 1)
                    yield

            def ret(p):
                dist = TB[:, T_DIST:T_DIST + 2 * TOK]
                act.wait_ge(lg_done, 1)
                for h in range(HEADS0 + 1):
                    if h < HEADS0:
                        act.wait_ge(rt_arg, HEADS0 * p + h + 1)
                        if p == 0:
                            if h >= 2:
                                act.wait_ge(rt_m, h - 1)
                            nc.scalar.activation(DC[:, h % 2, :], DT[:, 0, :], ACT.Exp).then_inc(rt_exp, 1)
                        else:
                            if h >= 1:
                                act.wait_ge(rt_m, RET[1] + 2 * h)
                            nc.scalar.activation(DC[:, 0, :], DT[:, 0, :], ACT.Exp)
                            nc.scalar.activation(DC[:, 1, :], dist, ACT.Exp, scale=LG[:, 0, h:h + 1], bias=LG[:, 2, h:h + 1])
                            nc.scalar.activation(DT[:, 1, :], dist, ACT.Exp, scale=LG[:, 1, 8 + h:9 + h],
                                                 bias=LG[:, 2, 8 + h:9 + h]).then_inc(rt_exp, 1)
                    yield
                act.wait_ge(rt_var, p + 1)
                nc.scalar.activation(gst[:, 2, :, :], gst[:, 1, :, :], ACT.Sqrt).then_inc(rt_sd, 1)
                yield

            def outp(p):
                l, tl = PASS[p]
                nt, t0 = len(tl), T_OF[p]
                yield
                for n in range(2 * nt):
                    t, q = tl[n // 2], n % 2
                    act.wait_ge(op_tr, 2 * t0 + n + 1)
                    if n == 0 and p < 3:
                        act.dma_start(SK, a["subk"][l]).then_inc(sk_in, 16)
                    nc.scalar.activation(HT[:, 4 * q:4 * q + 4, (t % 2) * P:(t % 2 + 1) * P],
                                         PS[:, 2 + n % 2, :].rearrange("p (c n) -> p c n", c=4), ACT.Copy).then_inc(op_ev, 1)
                    yield
                for u in range(2 * nt):
                    yield

            def prep(p):
                l, tl = PASS[p]
                nt, t0 = len(tl), T_OF[p]
                for _ in range(3):
                    yield
                root("n2", p, tl)
                yield
                for n in range(2 * nt):
                    t, q = tl[n // 2], n % 2
                    act.wait_ge(n2_tr, 2 * t0 + n + 1)
                    nc.scalar.activation(HT[:, 4 * q:4 * q + 4, (t % 2) * P:(t % 2 + 1) * P],
                                         PS[:, 2 + n % 2, :].rearrange("p (c n) -> p c n", c=4), ACT.Copy).then_inc(n2_ev, 1)
                    yield
                for hp in range(17):
                    if hp < 16:
                        act.wait_ge(pq_mm, 16 * p + hp + 1)
                        if hp >= 2:
                            act.wait_ge(ps_mm, 16 * p + hp - 1)
                        nc.scalar.activation(QTB[:, hp % 2, 0:nt * P], PS[:, hp % 2, 0:nt * P], ACT.Copy).then_inc(pq_ev, 1)
                    yield

            def exps(g):
                act.wait_ge(routed, g + 1)
                if g >= NR:
                    act.wait_ge(w_ready, g - NR + 1)
                nc.scalar.activation(EXPS[:, g % NR, :], BEST[:, g % NR, :], ACT.Exp, bias=EZ[:, 0, g % NR:g % NR + 1],
                                     accum_out=EZ[:, 1, g % NR:g % NR + 1]).then_inc(exps_done, 1)

            def gathers(T0, T1_, steps):
                exps(8 * T0)
                exps(8 * T0 + 1)
                for slot in range(S1 * T0, S1 * T1_ + LAG):
                    s = slot - LAG
                    if slot % TOPK == 0 and S1 * T0 < slot <= S1 * T1_:
                        g = slot // TOPK - 1
                        act.wait_ge(u_dot, slot)
                        nc.scalar.activation(av_[:, 1, g % 2, :], av_[:, 0, g % 2, :], ACT.Gelu).then_inc(act_done, 1)
                    g, j = divmod(s, TOPK)
                    steps_at(T0, slot, steps)
                    if s < S1 * T0:
                        continue
                    if j == 0:
                        act.wait_ge(w_ready, g + 1)
                    if s >= NV:
                        act.wait_ge(v_used, s - NV + 1)
                    nc.scalar.activation(diag[:, j % NV, :], ident, ACT.Copy, scale=av_[:, 2, g % 2, j:j + 1]).then_inc(dg_ready, 1)
                    if j == TOPK - 1 and g + 2 < 8 * T1_:
                        exps(g + 2)
                assert next(steps, "end") == "end"

            act.dma_start(X[:, 0:2, :], a["x"].rearrange("b (t p) d -> p (b t) d", p=P)).then_inc(ld_x, 16)
            act.dma_start(X[:, 2:4, :], a["ctx"].rearrange("b (t p) d -> p (b t) d", p=P)).then_inc(ld_x, 16)
            for n, name in enumerate(["na_q_norm", "na_k_norm", "swa_q_norm", "swa_k_norm"]):
                act.dma_start(gains[:, n, :], a[name].broadcast_to([P, HD])).then_inc(ld_g, 16)
            act.dma_start(LG[:, 3, :], a["ret_log_decay"].rearrange("a b c -> a (b c)").broadcast_to([P, 16])).then_inc(ld_g, 16)
            act.dma_start(sink[:, 0, :], a["swa_sink"].broadcast_to([P, HEADS1])).then_inc(ld_g, 16)
            act.wait_ge(setup_t, 2)
            nc.scalar.activation(SC[:, :, :], PS[:, 7, 0:16].rearrange("p (c k) -> p c k", c=2), ACT.Silu).then_inc(setup_sc, 1)
            act.wait_ge(ld_g, 96)
            nc.scalar.activation(LG[:, 0, :], LG[:, 3, :], ACT.Exp).then_inc(lg_e, 1)
            act.wait_ge(ld_x, 32)
            for _ in chain(ada(0, range(4)), norm1(0), proj(0), beside(chain(attn(0), ret(0)), ada(0, range(4, 12))), outp(0)):
                pass
            rest = ready(0, prep(0))
            gathers(0, 4, chain(rest, norm1(1), proj(1), attn(1), ret(1), outp(1), prep(1),
                                ada(1, range(12)), norm1(2), proj(2), norm1(3), proj(3)))
            for _ in chain(norm1(4), proj(4), attn(2), outp(2)):
                pass
            rest = ready(2, prep(2))
            gathers(4, 6, chain(rest, attn(3), outp(3), prep(3)))

        @block.vector
        def _(v):
            count = [0]

            def link(ins):
                count[0] += 1
                ins.then_inc(dv, 1)
                v.wait_ge(dv, count[0])

            def rms(which, n, tl, junk):
                for t in tl:
                    ins = nc.vector.tensor_tensor_reduce(junk(t), X[:, t, :], X[:, t, :], 1.0, 0.0, ALU.mult, ALU.add,
                                                         st[:, 0, t:t + 1])
                link(ins)
                lo, hi = tl[0], tl[-1] + 1
                nc.vector.tensor_scalar(st[:, 1, lo:hi], st[:, 0, lo:hi], 1.0 / D, 1e-6, ALU.mult, ALU.add).then_inc(n_ms, 1)
                v.wait_ge(n_rt, RMS[which, n] + 1)
                nc.vector.reciprocal(st[:, 3, lo:hi], st[:, 2, lo:hi]).then_inc(n_rs, 1)
                v.wait_ge(n_rs, RMS[which, n] + 1)

            def row(dst, p, which):
                n = ROW[p, which]
                v.wait_ge(row_mm, n + 1)
                nc.vector.tensor_copy(dst, PS[:, 4:6, :].rearrange("p b n -> p (b n)")).then_inc(row_ev, 1)

            def mod_cols(l, b0, b1):
                v.wait_ge(mod_tr, 12 * l + b1)
                j0, j1 = 4 * b0, 4 * b1
                link(nc.vector.tensor_tensor(MC[l][:, j0:j1, :], MT(l)[:, 2 * j0:2 * j1].rearrange("p (j c) -> p j c", c=2),
                                             VC[:, 48 * l + j0:48 * l + j1].unsqueeze(2).broadcast_to([P, j1 - j0, 2]), ALU.add))
                for at, gn in ((8, 96 + 8 * l), (32, 112 + 8 * l)):
                    if not j0 <= at < j1:
                        continue
                    ins = nc.vector.scalar_tensor_tensor(
                        out=MC[l][:, at:at + 8, :], in0=MC[l][:, at:at + 8, :], scalar=1.0,
                        in1=VC[:, gn:gn + 8].unsqueeze(2).broadcast_to([P, 8, 2]), op0=ALU.add, op1=ALU.mult)
                ins.then_inc(mc_done, 1)

            def ada(l, bs):
                for _ in range(2 * len(bs)):
                    yield
                mod_cols(l, bs[0], bs[-1] + 1)
                yield

            def norm1(j):
                l, tl = NORM[j]
                nt = len(tl)
                rms("n1", j, tl, lambda t: XN[:, t % 2, :])
                yield
                v.wait_ge(*[(mc_done, 1), (pq_mm, 16), (pq_mm, 32), (pr_mm, U_OF[2][1]), (pr_mm, U_OF[3][1])][j])
                v.wait_ge(mc_done, l + 2 if j else 1)
                c = tl[0] // 2
                lo = (tl[0] % 2) * P
                for m in range(4):
                    v.wait_ge(n1_tr, 4 * j + m + 1)
                    for kk in range(2):
                        k = 2 * m + kk
                        ins = nc.vector.tensor_scalar(HT[:, k, lo:lo + nt * P], PS[:, 2 + m % 2, kk * nt * P:(kk + 1) * nt * P],
                                                      MC[l][:, 8 + k, c:c + 1], MC[l][:, k, c:c + 1], ALU.mult, ALU.add)
                    ins.then_inc(n1_ev, 1)
                    yield

            def part_a(u):
                n = normed[u]
                nh = 4 if UNITS[u][3] == "kv" else 8
                v.wait_ge(pr_sq, n + 1)
                if nh < 8:
                    nc.vector.memset(nst[:, n % 2, 2, nh:8], 1.0)
                link(nc.vector.tensor_reduce(nst[:, n % 2, 2, 0:nh], SQ[:, n % 2, 0:nh * HD].rearrange("p (h d) -> p h d", d=HD),
                                             AX, ALU.add))
                nc.vector.tensor_scalar(nst[:, n % 2, 0, :], nst[:, n % 2, 2, :], 1.0 / HD, 1e-6, ALU.mult, ALU.add)\
                  .then_inc(pr_ms, 1)

            def free_psum(u, ins):
                ins.then_inc(pr_free, 1)
                v.wait_ge(pr_free, u + 1)

            def heads(x):
                return x.rearrange("p (h d) -> p h d", d=HD)

            def rotated(src, nh, t):
                r0 = T_ROPE + 96 * t
                cos = TB[:, r0:r0 + 32].unsqueeze(1).unsqueeze(1).broadcast_to([P, nh, 2, 32])
                nsin = TB[:, r0 + 32:r0 + 64].unsqueeze(1).broadcast_to([P, nh, 32])
                sin = TB[:, r0 + 64:r0 + 96].unsqueeze(1).broadcast_to([P, nh, 32])
                s4 = src.rearrange("p (h e d) -> p h e d", e=2, d=32)
                t1 = T1[:, 0:nh * HD].rearrange("p (h e d) -> p h e d", e=2, d=32)
                t2 = T2[:, 0:nh * HD].rearrange("p (h e d) -> p h e d", e=2, d=32)
                nc.vector.tensor_tensor(t1, s4, cos, ALU.mult)
                nc.vector.tensor_tensor(t2[:, :, 0, :], s4[:, :, 1, :], nsin, ALU.mult)
                return nc.vector.tensor_tensor(t2[:, :, 1, :], s4[:, :, 0, :], sin, ALU.mult)

            def part_b(u):
                l, g, t, kind = UNITS[u]
                ps = PS[:, (0, 1, 4)[u % 3], :]
                nn, nq = normed[u], turned[u]
                if kind in ("v", "rv", "gate"):
                    v.wait_ge(pr_mm, u + 1)
                    dst = O[:, t % 2, 512:1024] if kind == "gate" else VA[:, int(kind == "rv"), t, :]
                    nc.vector.tensor_copy(dst, ps).then_inc(pr_free, 1)
                    return
                if nq >= 2:
                    v.wait_ge(pr_tr, nq - 1)
                if nq >= 1:
                    v.wait_ge(pr_qn, nq)
                qn = QN[:, nq % 2, :]
                if kind in ("rq", "rk"):
                    v.wait_ge(pr_mm, u + 1)
                    if t < 2:
                        free_psum(u, rotated(ps, 8, t))
                    else:
                        free_psum(u, nc.vector.tensor_copy(T1, ps))
                        nc.vector.memset(T2, 0.0)
                    v.wait_ge(pr_free, u + 1)
                    if t >= 2:
                        nc.vector.tensor_copy(qn, T1).then_inc(pr_qn, 1)
                    else:
                        nc.vector.tensor_tensor(qn, T1, T2, ALU.add).then_inc(pr_qn, 1)
                    return
                nh = 4 if kind == "kv" else 8
                gain = gains[:, 2 * l + (0 if kind == "q" else 1), :]
                gb = gain.unsqueeze(1).broadcast_to([P, nh, HD])
                v.wait_ge(pr_rt, nn + 1)
                link(nc.vector.reciprocal(nst[:, nn % 2, 1, 0:nh], nst[:, nn % 2, 1, 0:nh]))
                if kind == "kv":
                    nc.vector.tensor_copy(V1[:, t, :], ps[:, 256:512])
                free_psum(u, nc.vector.tensor_tensor(heads(T2[:, 0:nh * HD]), heads(ps[:, 0:nh * HD]),
                                                     nst[:, nn % 2, 1, 0:nh].unsqueeze(2).broadcast_to([P, nh, HD]), ALU.mult))
                if l == 0:
                    nc.vector.tensor_tensor(heads(qn), heads(T2), gb, ALU.mult).then_inc(pr_qn, 1)
                    return
                base = SQ[:, nn % 2, 0:nh * HD]
                link(nc.vector.tensor_tensor(heads(base), heads(T2[:, 0:nh * HD]), gb, ALU.mult))
                if t < 2:
                    link(rotated(base, nh, t))
                if kind == "q":
                    nc.vector.tensor_tensor(qn, T1, T2, ALU.add).then_inc(pr_qn, 1)
                    return
                q4 = qn.rearrange("p (h e d) -> p h e d", e=2, d=HD)
                for e in range(2):
                    if t < 2:
                        ins = nc.vector.tensor_tensor(q4[:, :, e, :], heads(T1[:, 0:256]), heads(T2[:, 0:256]), ALU.add)
                    else:
                        ins = nc.vector.tensor_copy(q4[:, :, e, :], heads(base))
                ins.then_inc(pr_qn, 1)

            def proj(j):
                u0, u1 = U_OF[j]
                for u in range(u0, u1 + 2):
                    if u < u1 and UNITS[u][3] in NORMED:
                        part_a(u)
                    if u0 <= u - 1 < u1:
                        part_b(u - 1)
                    yield

            def attn(p):
                i0, i1 = I_OF[p]
                l = PASS[p][0]
                for i in range(i0, i1 + 2):
                    if i < i1:
                        _, h, t = ITEMS[i]
                        nk = TOK if t >= 2 else 2 * TOK
                        v.wait_ge(at_s, i + 1)
                        ins = nc.vector.tensor_reduce(sums[:, 1, i:i + 1], PS[:, i % 2, 0:nk], AX, ALU.max, negate=True)
                        if l == 1:
                            link(ins)
                            ins = nc.vector.tensor_tensor(sums[:, 1, i:i + 1], sums[:, 1, i:i + 1], sink[:, 1, h:h + 1], ALU.min)
                        ins.then_inc(at_max, 1)
                    if i0 <= i - 1 < i1:
                        m = i - 1
                        nk = TOK if ITEMS[m][2] >= 2 else 2 * TOK
                        v.wait_ge(at_tr, m + 1)
                        if m >= 2:
                            v.wait_ge(at_pv, m - 1)
                        nc.vector.tensor_copy(PT[:, m % 2, 0:nk // P, :], PS[:, 2 + m % 2, 0:nk].rearrange("p (k n) -> p k n", n=P))\
                          .then_inc(at_pT, 1)
                    if i - 2 >= i0:
                        m = i - 2
                        _, h, t = ITEMS[m]
                        v.wait_ge(at_pv, m + 1)
                        if l == 1:
                            link(nc.vector.tensor_tensor(sums[:, 3, m:m + 1], sums[:, 0, m:m + 1], sums[:, 2, m:m + 1], ALU.add))
                        link(nc.vector.reciprocal(sums[:, 4, m:m + 1], sums[:, 3 if l else 0, m:m + 1]))
                        nc.vector.tensor_scalar(O[:, t % 2, h * HD:(h + 1) * HD], PS[:, 4 + m % 2, 0:HD], sums[:, 4, m:m + 1],
                                                None, ALU.mult).then_inc(at_o, 1)
                    yield

            def decay_arg(p, h):
                dist = TB[:, T_DIST:T_DIST + 2 * TOK]
                n = HEADS0 * p + h
                if n >= 1:
                    v.wait_ge(rt_exp, n)
                nc.vector.tensor_scalar(DT[:, 0, :], dist, 0.0, LG[:, 0, h:h + 1], ALU.max, ALU.mult)
                link(nc.vector.tensor_scalar(DT[:, 1, :], dist, 0.0, LG[:, 1, 8 + h:9 + h], ALU.min, ALU.mult))
                nc.vector.tensor_tensor(DT[:, 0, :], DT[:, 0, :], DT[:, 1, :], ALU.add).then_inc(rt_arg, 1)

            def ret(p):
                per = p + 1
                v.wait_ge(at_pv, I_OF[p][1])
                v.wait_ge(at_s, I_OF[p][1])
                decay_arg(p, 0)
                for h in range(HEADS0 + 1):
                    if h < HEADS0:
                        v.wait_ge(rt_exp, HEADS0 * p + h + 1)
                        if p == 1:
                            link(nc.vector.tensor_tensor(DC[:, 1, :], DC[:, 1, :], DT[:, 1, :], ALU.add))
                        if h + 1 < HEADS0:
                            decay_arg(p, h + 1)
                        if h >= 2:
                            v.wait_ge(rt_pv, HEADS0 * p + h - 1)
                        for w in range(per):
                            v.wait_ge(rt_s, RET[p] + per * h + w + 1)
                            nc.vector.tensor_tensor(ST[:, h % 2, w, :], PS[:, 2 * (h % 2) + w, :],
                                                    DC[:, h % 2 if p == 0 else w, :], ALU.mult).then_inc(rt_m, 1)
                    yield
                v.wait_ge(rt_pv, HEADS0 * (p + 1))
                v.wait_ge(rt_m, RET[p + 1])
                v.wait_ge(pr_gate, p + 1)
                for t in range(2):
                    link(nc.vector.tensor_reduce(gst[:, 0, t, :], heads(PS[:, 4 + t, :]), AX, ALU.add))
                link(nc.vector.tensor_scalar(gst[:, 0, :, :], gst[:, 0, :, :], 1.0 / HD, None, ALU.mult))
                for t in range(2):
                    oc = heads(OC[:, t, :])
                    link(nc.vector.tensor_tensor(oc, heads(PS[:, 4 + t, :]), gst[:, 0, t, :].unsqueeze(2).broadcast_to([P, 8, HD]),
                                                 ALU.subtract))
                    link(nc.vector.tensor_tensor(DT[:, 0, :], OC[:, t, :], OC[:, t, :], ALU.mult))
                    link(nc.vector.tensor_reduce(gst[:, 3, t, :], heads(DT[:, 0, :]), AX, ALU.add))
                nc.vector.tensor_scalar(gst[:, 1, :, :], gst[:, 3, :, :], 1.0 / HD, 1e-5, ALU.mult, ALU.add).then_inc(rt_var, 1)
                v.wait_ge(rt_sd, p + 1)
                link(nc.vector.reciprocal(gst[:, 3, :, :], gst[:, 2, :, :]))
                for t in range(2):
                    oc = heads(OC[:, t, :])
                    link(nc.vector.tensor_tensor(oc, oc, gst[:, 3, t, :].unsqueeze(2).broadcast_to([P, 8, HD]), ALU.mult))
                    nc.vector.tensor_tensor(O[:, t, 512:1024], OC[:, t, :], O[:, t, 512:1024], ALU.mult).then_inc(rt_o, 1)
                v.wait_ge(rt_o, 2 * p + 2)
                yield

            def outp(p):
                l, tl = PASS[p]
                nt, t0 = len(tl), T_OF[p]
                v.wait_ge(at_tr, I_OF[p][1])
                row(G1, p, "g1")
                yield
                for n in range(2 * nt):
                    yield
                v.wait_ge(row_ev, ROW[p, "g1"] + 1)
                for u in range(2 * nt):
                    b, t = u // nt, tl[u % nt]
                    v.wait_ge(op_mm, 2 * t0 + u + 1)
                    xs = X[:, t, b * BLK:(b + 1) * BLK]
                    link(nc.vector.tensor_tensor(YT[:, u % 2, :], PS[:, u % 2, :], G1[:, b * BLK:(b + 1) * BLK], ALU.mult))
                    nc.vector.tensor_tensor(xs, xs, YT[:, u % 2, :], ALU.add).then_inc(op_x, 1)
                    v.wait_ge(op_x, 2 * t0 + u + 1)
                    yield

            def prep(p):
                l, tl = PASS[p]
                nt, t0 = len(tl), T_OF[p]
                if (p, "g2") in ROW:
                    if p == 2:
                        v.wait_ge(tile_added, 2)
                    row(G2[:, (0, 1, 0)[p], :], p, "g2")
                yield
                row(ROWS2[:, 0, :], p, "A2")
                yield
                row(ROWS2[:, 1, :], p, "sh2")
                yield
                v.wait_ge(row_ev, ROW[p, "sh2"] + 1)
                if t0 + nt > 3:
                    v.wait_ge(u_dot, S1 * (t0 + nt - 3))
                rms("n2", p, tl, lambda t: H2[:, (t0 + tl.index(t)) % 3, :])
                for e, t in enumerate(tl):
                    h2 = H2[:, (t0 + e) % 3, :]
                    link(nc.vector.scalar_tensor_tensor(out=h2, in0=X[:, t, :], scalar=st[:, 3, t:t + 1],
                                                        in1=ROWS2[:, 0, :], op0=ALU.mult, op1=ALU.mult))
                    nc.vector.tensor_tensor(h2, h2, ROWS2[:, 1, :], ALU.add).then_inc(n2_h, 1)
                v.wait_ge(n2_h, t0 + nt)
                yield
                for n in range(2 * nt):
                    yield
                for hp in range(17):
                    if hp >= 1:
                        m = hp - 1
                        v.wait_ge(ps_mm, 16 * p + m + 1)
                        todo = [(PS[:, 2 + m % 2, e * P:(e + 1) * P], TOPV[:, (t0 + e) % 3, m, :], TOPI[:, (t0 + e) % 3, m, :],
                                 spare[:, e, :]) for e in range(nt)]
                        for s, tv, ti, sp_ in todo:
                            ins = nc.vector.max(tv[:, 0:8], s)
                        link(ins)
                        for s, tv, ti, sp_ in todo:
                            nc.vector.max_index(ti[:, 0:8], tv[:, 0:8], s)
                            ins = nc.vector.match_replace(sp_, tv[:, 0:8], s, LOWEST)
                        link(ins)
                        for s, tv, ti, sp_ in todo:
                            ins = nc.vector.max(tv[:, 8:16], sp_)
                        link(ins)
                        for s, tv, ti, sp_ in todo:
                            ins = nc.vector.max_index(ti[:, 8:16], tv[:, 8:16], sp_)
                        ins.then_inc(tp_done, 1)
                        v.wait_ge(tp_done, 16 * p + m + 1)
                    yield

            def route(g):
                T, h = divmod(g, 8)
                vals, idx = TOPV[:, T % 3, 2 * h:2 * h + 2, :], TOPI[:, T % 3, 2 * h:2 * h + 2, :]
                best = BEST[:, g % NR, :]
                if g >= 1:
                    v.wait_ge(routed, g)
                if g >= NR:
                    v.wait_ge(exps_done, g - NR + 1)
                    v.wait_ge(v_used, TOPK * (g - NR + 1))
                nc.vector.tensor_copy(rf[:, 0:2, :], idx)
                cand = rc[:, 0, :].rearrange("p (i j) -> p i j", j=TOPK)
                link(nc.vector.tensor_tensor(cand, vals[:, 0, :].unsqueeze(2).broadcast_to([P, TOPK, TOPK]),
                                             vals[:, 1, :].unsqueeze(1).broadcast_to([P, TOPK, TOPK]), ALU.add))
                link(nc.vector.max(best[:, 0:8], rc[:, 0, :]))
                nc.vector.tensor_scalar(EZ[:, 0, g % NR:g % NR + 1], best[:, 0:1], -1.0, None, ALU.mult)
                nc.vector.max_index(ri[:, 0, 0:8], best[:, 0:8], rc[:, 0, :])
                link(nc.vector.match_replace(rc[:, 1, :], best[:, 0:8], rc[:, 0, :], LOWEST))
                link(nc.vector.max(best[:, 8:16], rc[:, 1, :]))
                link(nc.vector.max_index(ri[:, 0, 8:16], best[:, 8:16], rc[:, 1, :]))
                nc.vector.tensor_single_scalar(ri[:, 1, :], ri[:, 0, :], 4, ALU.logical_shift_right)
                link(nc.vector.tensor_single_scalar(ri[:, 2, :], ri[:, 0, :], TOPK - 1, ALU.bitwise_and))
                link(nc.vector.tensor_copy(rf[:, 2:4, :], ri[:, 1:3, :]))
                for p in range(2):
                    oh = rc[:, p, :].rearrange("p (s k) -> p s k", k=TOPK)
                    ins = nc.vector.tensor_tensor(oh, rf[:, 2 + p, :].unsqueeze(2).broadcast_to([P, TOPK, TOPK]),
                                                  TB[:, T_IOTA:T_END].unsqueeze(1).broadcast_to([P, TOPK, TOPK]), ALU.is_equal)
                link(ins)
                for p in range(2):
                    oh = rc[:, p, :].rearrange("p (s k) -> p s k", k=TOPK)
                    ins = nc.vector.tensor_tensor(oh, oh, rf[:, p, :].unsqueeze(1).broadcast_to([P, TOPK, TOPK]), ALU.mult)
                link(ins)
                link(nc.vector.tensor_reduce(rf[:, 2:4, :], rc[:, :, :].rearrange("p b (s k) -> p b s k", k=TOPK), AX, ALU.add))
                nc.vector.scalar_tensor_tensor(out=IDX[:, g % NR, :], in0=rf[:, 2, :], scalar=float(P), in1=rf[:, 3, :],
                                               op0=ALU.mult, op1=ALU.add).then_inc(routed, 1)

            def weigh(g):
                v.wait_ge(exps_done, g + 1)
                link(nc.vector.reciprocal(EZ[:, 2, g % NR:g % NR + 1], EZ[:, 1, g % NR:g % NR + 1]))
                v.wait_ge(act_done, g + 1)
                if g >= 2:
                    v.wait_ge(dg_ready, TOPK * (g - 1))
                nc.vector.scalar_tensor_tensor(out=av_[:, 2, g % 2, :], in0=av_[:, 1, g % 2, :], scalar=EZ[:, 2, g % NR:g % NR + 1],
                                               in1=EXPS[:, g % NR, :], op0=ALU.mult, op1=ALU.mult).then_inc(w_ready, 1)

            def add_tile(T):
                t = TILE[T][1]
                v.wait_ge(v_used, S1 * (T + 1))
                for e in range(2):
                    cols = slice(e * 512, (e + 1) * 512)
                    link(nc.vector.tensor_tensor(TMP[:, :], PS[:, 6 + e, :], G2[:, (0, 0, 1, 1, 0, 0)[T], cols], ALU.mult))
                    ins = nc.vector.tensor_tensor(X[:, t, cols], X[:, t, cols], TMP[:, :], ALU.add)
                    if e == 0:
                        link(ins)
                ins.then_inc(tile_added, 1)
                v.wait_ge(tile_added, T + 1)

            def gathers(T0, T1_, steps):
                route(8 * T0)
                route(8 * T0 + 1)
                for slot in range(S1 * T0, S1 * T1_ + LAG):
                    steps_at(T0, slot, steps)
                    if slot % TOPK == 1 and S1 * T0 + TOPK < slot <= S1 * T1_ + 1:
                        weigh(slot // TOPK - 1)
                    if slot % S1 == LAG and slot - S1 >= S1 * T0 and slot < S1 * T1_:
                        add_tile(slot // S1 - 1)
                    if slot >= S1 * T1_:
                        continue
                    g, j = divmod(slot, TOPK)
                    v.wait_ge(u_in[j % NU], 16 * (slot // NU + 1))
                    if j == 0 and g >= 2:
                        v.wait_ge(act_done, g - 1)
                    nc.vector.tensor_tensor_reduce(UB[:, j % NU, :], UB[:, j % NU, :], H2[:, g // 8 % 3, :], 1.0, 0.0,
                                                   ALU.mult, ALU.add, av_[:, 0, g % 2, j:j + 1]).then_inc(u_dot, 1)
                    if j == TOPK - 1:
                        if g + 2 < 8 * T1_:
                            route(g + 2)
                assert next(steps, "end") == "end"
                add_tile(T1_ - 1)

            v.wait_ge(setup_t, 1)
            link(nc.vector.tensor_copy(VC[:, :], PS[:, 6, 0:P]))
            v.wait_ge(lg_e, 1)
            link(nc.vector.tensor_scalar(LG[:, 1, :], LG[:, 0, :], 1.0, None, ALU.mult))
            link(nc.vector.tensor_scalar(LG[:, 2, :], LG[:, 0, :], -float(TOK), None, ALU.mult))
            link(nc.vector.tensor_scalar(LG[:, 0, :], LG[:, 0, :], -1.0, None, ALU.mult))
            nc.vector.tensor_scalar(sink[:, 1, :], sink[:, 0, :], -1.0, None, ALU.mult).then_inc(lg_done, 1)
            v.wait_ge(ld_x, 32)
            v.wait_ge(ld_g, 96)
            n0 = norm1(0)
            next(n0)
            mod_cols(0, 0, 4)
            for _ in chain(n0, proj(0), beside(chain(attn(0), ret(0)), ada(0, range(4, 12))), outp(0)):
                pass
            rest = ready(0, prep(0))
            gathers(0, 4, chain(rest, norm1(1), proj(1), attn(1), ret(1), outp(1), prep(1),
                                ada(1, range(12)), norm1(2), proj(2), norm1(3), proj(3)))
            for _ in chain(norm1(4), proj(4), attn(2), outp(2)):
                pass
            rest = ready(2, prep(2))
            gathers(4, 6, chain(rest, attn(3), outp(3), prep(3)))


_INS = ["x", "c", "ctx", "c_ctx", "mod_w", "mod_b", "norm1_g", "norm2_g", "ab_w_in", "ab_w_out", "na_q_norm",
        "na_k_norm", "ret_log_decay", "swa_w_in", "swa_w_out", "swa_q_norm", "swa_k_norm", "swa_sink",
        "peer_w_q"]


def kernel(**inputs):
    import concourse.bacc as _bacc
    from concourse.bass_utils import run_bass_kernel_spmd as _run

    nc = _bacc.Bacc("TRN2", target_bir_lowering=False, num_devices=1)
    laid = {name: np.asarray(inputs[name]) for name in _INS}
    laid["table"] = constant_table()
    rpb = np.asarray(inputs["na_rpb"])[0]
    dr, dc = bias_places()
    padded = np.concatenate([rpb, np.full(rpb.shape[:2] + (1,), NEG, rpb.dtype)], axis=2)
    laid["nab"] = padded[:, dr, dc]
    sk = np.asarray(inputs["peer_sub_keys"])
    laid["subk"] = np.ascontiguousarray(sk.transpose(0, 4, 1, 2, 3)).reshape(2, P, 16, P)
    for l in range(2):
        laid[f"peer_u{l}"] = np.asarray(inputs["peer_u"])[l]
        laid[f"peer_v{l}"] = np.asarray(inputs["peer_v"])[l]
    arrays, aps = {}, {}
    for name, arr in laid.items():
        arr = np.ascontiguousarray(arr)
        arrays[f"in_{name}"] = arr
        aps[name] = nc.dram_tensor(f"in_{name}", arr.shape, mybir.dt.from_np(arr.dtype), kind="ExternalInput").ap()
    out = nc.dram_tensor("out_0", (1, TOK, D), F32, kind="ExternalOutput").ap()
    backbone(nc, aps, out)
    r = _run(nc, [arrays], core_ids=[0])
    return r.results[0]["out_0"]
```
